# Optimizing a Trainium2 kernel written in Bass

```python
import jax, jax.numpy as jnp
from jax import lax
import numpy as np

D_MODEL = 1024
BATCH = 1
SEQ = 256
DEPTH = 2

HEAD_DIM = 64
MOBA_HEADS = 8
SWA_HEADS = 8
SWA_KV_HEADS = 2
MOBA_WIDTH = MOBA_HEADS * HEAD_DIM
SWA_WIDTH = SWA_HEADS * HEAD_DIM
SWA_KV_WIDTH = SWA_KV_HEADS * HEAD_DIM
MIX_WIDTH = MOBA_WIDTH + SWA_WIDTH
IN_WIDTH = 3 * MOBA_WIDTH + SWA_WIDTH + 2 * SWA_KV_WIDTH
MOBA_BLOCK = 256
MOBA_TOPK = 3
MOBA_Q_CHUNK = 32
SWA_WINDOW = 128
D_FF = -(-8 * D_MODEL // (3 * 256)) * 256
ROPE_THETA = 10000.0
EPS = 1e-6
NEG_INF = -1e30
SPLIT_OFFSETS = [MOBA_WIDTH, 2 * MOBA_WIDTH, 3 * MOBA_WIDTH,
                 3 * MOBA_WIDTH + SWA_WIDTH, 3 * MOBA_WIDTH + SWA_WIDTH + SWA_KV_WIDTH]

kernel_name = "hymba_moba_swa_sink_sandwich_trunk"

def rms_norm(x, g):
    xf = x.astype(jnp.float32)
    y = xf * lax.rsqrt(jnp.mean(xf * xf, axis=-1, keepdims=True) + EPS)
    return (y * g.astype(jnp.float32)).astype(x.dtype)

def rope_tables(seq):
    inv = 1.0 / (ROPE_THETA ** (jnp.arange(0, HEAD_DIM, 2, dtype=jnp.float32) / HEAD_DIM))
    ang = jnp.arange(seq, dtype=jnp.float32)[:, None] * inv[None, :]
    return jnp.cos(ang), jnp.sin(ang)

def apply_rope(x, cos, sin):
    x1, x2 = jnp.split(x.astype(jnp.float32), 2, axis=-1)
    c = cos[None, :, None, :]
    s = sin[None, :, None, :]
    return jnp.concatenate([x1 * c - x2 * s, x2 * c + x1 * s], axis=-1).astype(x.dtype)

def moba_attention(q, k, v):
    b, s, h, d = q.shape
    nb = -(-s // MOBA_BLOCK)
    pad = nb * MOBA_BLOCK - s
    scale = d ** -0.5
    qh = jnp.transpose(q, (0, 2, 1, 3))

    def to_blocks(a):
        a = jnp.pad(jnp.transpose(a, (0, 2, 1, 3)), ((0, 0), (0, 0), (0, pad), (0, 0)))
        return a.reshape(b, h, nb, MOBA_BLOCK, d)

    kb, vb = to_blocks(k), to_blocks(v)
    k_mean = jnp.mean(kb.astype(jnp.float32), axis=3)
    q_blk = jnp.arange(s) // MOBA_BLOCK
    gate = jnp.einsum('bhtd,bhnd->bhtn', qh.astype(jnp.float32), k_mean)
    fully_past = jnp.arange(nb)[None, :] < q_blk[:, None]
    gate = jnp.where(fully_past, gate, -jnp.inf)
    n_sel = min(MOBA_TOPK, nb)
    _, sel = lax.top_k(gate, n_sel)

    nc = s // MOBA_Q_CHUNK

    def to_chunks(a):
        a = a.reshape(a.shape[:2] + (nc, MOBA_Q_CHUNK) + a.shape[3:])
        return jnp.moveaxis(a, 2, 0)

    bi = jnp.arange(b)[:, None, None, None]
    hi = jnp.arange(h)[None, :, None, None]

    def chunk_fn(args):
        qc, selc, ci = args
        t = ci * MOBA_Q_CHUNK + jnp.arange(MOBA_Q_CHUNK)
        blk = t[0] // MOBA_BLOCK
        ks = kb[bi, hi, selc]
        vs = vb[bi, hi, selc]
        valid = jnp.arange(n_sel) < blk
        lp = jnp.einsum('bhcd,bhcjkd->bhcjk', qc, ks,
                        preferred_element_type=jnp.float32) * scale
        lp = jnp.where(valid[None, None, None, :, None], lp, NEG_INF)
        lp = lp.reshape(b, h, MOBA_Q_CHUNK, n_sel * MOBA_BLOCK)
        k_own = lax.dynamic_index_in_dim(kb, blk, axis=2, keepdims=False)
        v_own = lax.dynamic_index_in_dim(vb, blk, axis=2, keepdims=False)
        lo = jnp.einsum('bhcd,bhkd->bhck', qc, k_own,
                        preferred_element_type=jnp.float32) * scale
        kpos = blk * MOBA_BLOCK + jnp.arange(MOBA_BLOCK)
        lo = jnp.where(kpos[None, :] <= t[:, None], lo, NEG_INF)
        p = jax.nn.softmax(jnp.concatenate([lp, lo], axis=-1), axis=-1)
        pp = p[..., :n_sel * MOBA_BLOCK].reshape(b, h, MOBA_Q_CHUNK, n_sel, MOBA_BLOCK)
        po = p[..., n_sel * MOBA_BLOCK:]
        return (jnp.einsum('bhcjk,bhcjkd->bhcd', pp.astype(v.dtype), vs)
                + jnp.einsum('bhck,bhkd->bhcd', po.astype(v.dtype), v_own))

    o = lax.map(chunk_fn, (to_chunks(qh), to_chunks(sel), jnp.arange(nc)))
    o = jnp.moveaxis(o, 0, 2).reshape(b, h, s, d)
    return jnp.transpose(o, (0, 2, 1, 3))

def swa_sink_attention(q, k, v, sinks):
    b, s, hq, d = q.shape
    hkv = k.shape[2]
    g = hq // hkv
    w = SWA_WINDOW
    nblk = s // w
    scale = d ** -0.5
    qb = q.reshape(b, nblk, w, hkv, g, d)

    def band(a):
        ab = a.reshape(b, nblk, w, hkv, d)
        prev = jnp.pad(ab, ((0, 0), (1, 0), (0, 0), (0, 0), (0, 0)))[:, :-1]
        return jnp.concatenate([prev, ab], axis=2)

    kb, vb = band(k), band(v)
    logits = jnp.einsum('bnqhgd,bnphd->bhgnqp', qb, kb,
                        preferred_element_type=jnp.float32) * scale
    qpos = jnp.arange(nblk)[:, None, None] * w + jnp.arange(w)[None, :, None]
    kpos = jnp.arange(nblk)[:, None, None] * w - w + jnp.arange(2 * w)[None, None, :]
    diff = qpos - kpos
    mask = (diff >= 0) & (diff < w) & (kpos >= 0)
    logits = jnp.where(mask, logits, NEG_INF)
    sink = jnp.broadcast_to(sinks.astype(jnp.float32).reshape(hkv, g)[None, :, :, None, None, None],
                            logits.shape[:-1] + (1,))
    p = jax.nn.softmax(jnp.concatenate([logits, sink], axis=-1), axis=-1)[..., :-1]
    o = jnp.einsum('bhgnqp,bnphd->bnqhgd', p.astype(v.dtype), vb)
    return o.reshape(b, s, hq, d)

def hybrid_layer(x, cos, sin, w_in, b_in, w_out, g_attn_pre, g_attn_post, g_moba_out,
                 g_swa_out, sinks, g_ffn_pre, g_ffn_post, w_gate, w_up, w_down):
    b, s, _ = x.shape
    h = rms_norm(x, g_attn_pre)
    proj = jnp.einsum('bsd,de->bse', h, w_in) + b_in
    mq, mk, mv, sq, sk, sv = jnp.split(proj, SPLIT_OFFSETS, axis=-1)
    mq = apply_rope(mq.reshape(b, s, MOBA_HEADS, HEAD_DIM), cos, sin)
    mk = apply_rope(mk.reshape(b, s, MOBA_HEADS, HEAD_DIM), cos, sin)
    mv = mv.reshape(b, s, MOBA_HEADS, HEAD_DIM)
    sq = apply_rope(sq.reshape(b, s, SWA_HEADS, HEAD_DIM), cos, sin)
    sk = apply_rope(sk.reshape(b, s, SWA_KV_HEADS, HEAD_DIM), cos, sin)
    sv = sv.reshape(b, s, SWA_KV_HEADS, HEAD_DIM)
    mo = rms_norm(moba_attention(mq, mk, mv).reshape(b, s, MOBA_WIDTH), g_moba_out)
    so = rms_norm(swa_sink_attention(sq, sk, sv, sinks).reshape(b, s, SWA_WIDTH), g_swa_out)
    mix = jnp.concatenate([mo, so], axis=-1)
    x = x + rms_norm(jnp.einsum('bse,ed->bsd', mix, w_out), g_attn_post)
    h = rms_norm(x, g_ffn_pre)
    f = jax.nn.silu(jnp.einsum('bsd,df->bsf', h, w_gate)) * jnp.einsum('bsd,df->bsf', h, w_up)
    x = x + rms_norm(jnp.einsum('bsf,fd->bsd', f, w_down), g_ffn_post)
    return x

def setup_inputs(seed: int = 0) -> dict:
    key = jax.random.key(seed)
    ks = jax.random.split(key, 16)
    f32 = jnp.float32

    def nrm(k, shape, scale):
        return jax.random.normal(k, shape, f32) * scale

    def gain(k, width):
        return 1.0 + 0.05 * jax.random.normal(k, (DEPTH, width), f32)

    return {
        "x": jax.random.normal(ks[0], (BATCH, SEQ, D_MODEL), f32),
        "w_in": nrm(ks[1], (DEPTH, D_MODEL, IN_WIDTH), D_MODEL ** -0.5),
        "b_in": nrm(ks[2], (DEPTH, IN_WIDTH), 0.02),
        "w_out": nrm(ks[3], (DEPTH, MIX_WIDTH, D_MODEL), MIX_WIDTH ** -0.5),
        "g_attn_pre": gain(ks[4], D_MODEL),
        "g_attn_post": gain(ks[5], D_MODEL),
        "g_moba_out": gain(ks[6], MOBA_WIDTH),
        "g_swa_out": gain(ks[7], SWA_WIDTH),
        "attn_sinks": nrm(ks[8], (DEPTH, SWA_HEADS), 0.5),
        "g_ffn_pre": gain(ks[9], D_MODEL),
        "g_ffn_post": gain(ks[10], D_MODEL),
        "w_gate": nrm(ks[11], (DEPTH, D_MODEL, D_FF), D_MODEL ** -0.5),
        "w_up": nrm(ks[12], (DEPTH, D_MODEL, D_FF), D_MODEL ** -0.5),
        "w_down": nrm(ks[13], (DEPTH, D_FF, D_MODEL), D_FF ** -0.5),
    }

def reference(x, w_in, b_in, w_out, g_attn_pre, g_attn_post, g_moba_out, g_swa_out,
              attn_sinks, g_ffn_pre, g_ffn_post, w_gate, w_up, w_down):
    cos, sin = rope_tables(x.shape[1])
    for i in range(DEPTH):
        x = hybrid_layer(x, cos, sin, w_in[i], b_in[i], w_out[i], g_attn_pre[i], g_attn_post[i],
                         g_moba_out[i], g_swa_out[i], attn_sinks[i], g_ffn_pre[i], g_ffn_post[i],
                         w_gate[i], w_up[i], w_down[i])
    return x


_drawn_inputs = setup_inputs


def setup_inputs(seed=0):
    import zlib

    import numpy as np

    out = dict(_drawn_inputs(seed))
    spreads = {}
    factors = {'attn_sinks': 3.348}
    for name, (base, spread) in spreads.items():
        noise = np.random.default_rng([zlib.crc32(name.encode()), seed]).standard_normal(out[name].shape)
        drawn = base * np.exp(spread * noise) if base else spread * noise
        out[name] = __import__('jax').numpy.asarray(drawn.astype(out[name].dtype))
    for name, factor in factors.items():
        out[name] = (out[name] * factor).astype(out[name].dtype)
    return out
```

```python
from contextlib import ExitStack

import concourse.bass as bass
from concourse import mybir

F32 = mybir.dt.float32
F32R = mybir.dt.float32r
BF16 = mybir.dt.bfloat16
ACT = mybir.ActivationFunctionType
ALU = mybir.AluOpType
AX = mybir.AxisListType

P = 128
D = 1024
T = 2
SEQ = P * T
HEAD = 64
HEADS = 8
GROUP = HEADS * HEAD
KV = 2 * HEAD
IN = 4 * GROUP + 2 * KV
FF = 2816
BANK = 512
SCALE = HEAD ** -0.5
EPS = 1e-6
NEG = -1e30
MOBA, SWA = 0, 1

BLOCK = 2048
BLOCKS = [("in", 0, 8, 3 * GROUP + GROUP, 256)]
for col in (3 * GROUP, GROUP, 0, 2 * GROUP):
    BLOCKS += [("in", k, 4, col, BANK) for k in (0, 4)]
FIRST_OUT = len(BLOCKS)
BLOCKS += [("out", k, 4, col, BANK) for k in (4, 0) for col in (0, BANK)]
FIRST_FFN = len(BLOCKS)
FFN_CHUNKS = -(-FF // BANK)
for c in range(FF // BANK):
    BLOCKS += [(m, k, 4, c * BANK, BANK) for m in ("gate", "up") for k in (0, 4)]
BLOCKS += [(m, 0, 8, FF // BANK * BANK, 256) for m in ("gate", "up")]
FIRST_DOWN = len(BLOCKS)
KF = FF // P
BLOCKS += [("down", k, 2, 0, D) for k in range(0, KF, 2)]
NB = len(BLOCKS)
PROJ_COLS = [(4 * GROUP, 256), (3 * GROUP, BANK), (GROUP, BANK), (0, BANK), (2 * GROUP, BANK)]

RAW = 2
SLOTS = 4
SKIP_AT = 24
assert NB % RAW == 0


def slot(b):
    return b % SLOTS if b < SKIP_AT else (b - NB) % SLOTS


def before(b):
    c = b - 1
    while slot(c % NB) != slot(b):
        c -= 1
    return c


def freed_by(b):
    done = [c for c in range(NB + SLOTS) if max(before(x % NB) + x // NB * NB for x in range(c + 1)) <= b]
    last = [c for c in range(NB + SLOTS) if max(before(x % NB) + x // NB * NB for x in range(c + 1)) <= b - 1]
    return [c for c in done if c not in last]


def completes(b, t):
    m, k0, nk, col, n = BLOCKS[b]
    if m == "down":
        return [("down", t, c) for c in range(2)] if k0 + nk == KF else []
    if m == "out":
        return [("out", t, col // BANK)] if k0 == 0 else []
    if k0 + nk < D // P:
        return []
    return [("proj", (b + 1) // 2, t)] if m == "in" else [(m, col // BANK, t)]


ROUNDS = [(0, (0, 1, 2, 3)), (1, (0, 1)), (1, (2, 3))]


class Order:

    def __init__(self, names):
        self.names = list(names)
        self.at = {n: i for i, n in enumerate(self.names)}
        self.n = len(self.names)
        self.said = 0

    def tick(self, name):
        assert self.names[self.said % self.n] == name, (self.names[self.said % self.n], name)
        self.said += 1

    def before(self, L, name):
        return L * self.n + self.at[name]

    def done(self, L, name):
        return L * self.n + self.at[name] + 1


HOLDS = [[] for _ in range(8)]
for ci in range(5):
    for t in range(T):
        HOLDS[2 * (ci % 2) + t].append(("proj", ci, t))
for c in range(2):
    HOLDS[2 + c].append(("out", 0, c))
    HOLDS[c].append(("out", 1, c))
for c in range(FFN_CHUNKS):
    for t in range(T):
        HOLDS[2 - 2 * t].append(("gate", c, t))
        HOLDS[3 - 2 * t].append(("up", c, t))
for c in range(2):
    HOLDS[2 + c].append(("down", 0, c))
    HOLDS[c].append(("down", 1, c))
HOLDS[4] += [("ht", 0, 0, 1)] + [("scores", g, r, 0) for g in (SWA, MOBA) for r in range(3)] + [("ht", 1, 0, 1)]
HOLDS[5] += [("ht", 0, 1, 1)] + [("scores", g, r, 1) for g in (SWA, MOBA) for r in range(3)] + [("ht", 1, 1, 1)]
HOLDS[6] += [("ht", 0, 0, 0), ("qk", 0, 0), ("qk", 1, 0), ("qk", 0, 1), ("qk", 1, 1),
             ("pt", SWA, 0, 0), ("pt", SWA, 0, 1), ("qk", 2, 0), ("pt", SWA, 1, 0), ("pt", SWA, 1, 1),
             ("qk", 2, 1), ("qk", 3, 0), ("pt", SWA, 2, 0), ("pt", SWA, 2, 1), ("qk", 3, 1), ("mix", SWA, 0),
             ("pt", MOBA, 0, 0), ("mix", SWA, 1), ("pt", MOBA, 0, 1), ("pt", MOBA, 1, 0), ("mix", MOBA, 0),
             ("pt", MOBA, 1, 1), ("pt", MOBA, 2, 0), ("pt", MOBA, 2, 1), ("mix", MOBA, 1), ("ht", 1, 0, 0)]
HOLDS[6] += [("ft", c, 0) for c in range(FFN_CHUNKS)]
HOLDS[7] += [("ht", 0, 1, 0), ("pv", SWA, 0), ("pv", SWA, 1), ("pv", MOBA, 0), ("pv", MOBA, 1), ("ht", 1, 1, 0)]
HOLDS[7] += [("ft", c, 1) for c in range(FFN_CHUNKS)]
BANK_OF = {name: b for b in range(8) for name in HOLDS[b]}


def trunk(nc, x_in, w_in, b_in, w_out, g_attn_pre, g_attn_post, g_moba, g_swa, sinks_in,
          g_ffn_pre, g_ffn_post, w_gate, w_up, w_down, cos_in, sin_in, out):
    depth = w_in.shape[0]
    weights = {"in": w_in, "out": w_out, "gate": w_gate, "up": w_up, "down": w_down}

    with ExitStack() as ctx:
        def sb(name, shape, dt=F32):
            return ctx.enter_context(nc.sbuf_tensor(name, shape, dt))

        def sem(name):
            return ctx.enter_context(nc.semaphore(name))

        x = sb("x", [P, T, D])
        actT = {s: sb("actT_" + s, [P, D // P, SEQ], F32R) for s in "hl"}
        fT = {s: sb("fT_" + s, [P, KF, SEQ], F32R) for s in "hl"}
        raw = sb("raw", [P, RAW, BLOCK])
        w = {s: sb("w_" + s, [P, SLOTS, BLOCK], F32R) for s in "hl"}
        bias = sb("bias", [P, IN])
        gain_ffn = bias[:, 0:D]
        gain_a = sb("gain_a", [P, D])
        gain_b = sb("gain_b", [P, D])
        work = sb("work", [P, 11, BANK])
        stage = [work[:, t, :] for t in range(T)]
        roped = [work[:, 2 + t, :] for t in range(T)]
        probs = work[:, 4:6, :]
        probsT = work[:, 6:8, :]
        o = [work[:, 8 + t, :] for t in range(T)]
        rope_tmp = work[:, 10, :]
        y = [work[:, 0:2, :], work[:, 4:6, :]]
        silu = [work[:, 6 + t, :] for t in range(T)]
        f = [work[:, 8 + t, :] for t in range(T)]
        v = {MOBA: sb("v_moba", [P, T, GROUP]), SWA: sb("v_swa", [P, T, KV])}
        qT = {g: sb(f"qT_{g}", [P, 4, SEQ]) for g in (MOBA, SWA)}
        kT = {MOBA: sb("kT_0", [P, 4, SEQ]), SWA: sb("kT_1", [P, 1, SEQ])}
        ident = sb("ident", [P, P])
        ident16 = sb("ident16", [P, P], BF16)
        masks = sb("masks", [P, 4, P], BF16)
        cos = sb("cos", [P, T, HEAD // 2])
        sin = sb("sin", [P, T, HEAD // 2])
        sinks = sb("sinks", [P, 2, 4])
        neg_max = sb("neg_max", [P, 2, T, 2, 4])
        row_sum = sb("row_sum", [P, 2, T, 2, 4])
        top = sb("top", [P, 2, 4])
        sink_exp = sb("sink_exp", [P, 2, 4])
        norms = sb("norms", [P, 16])
        ss_x, rstd_x = norms[:, 0:2], norms[:, 2:4]
        ss_y, rstd_y = norms[:, 4:8].rearrange("p (t c) -> p t c", t=T), norms[:, 8:10]
        ss_o, rstd_o = norms[:, 10:12], norms[:, 12:14]
        constants = sb("constants", [P, 2])
        minus_half, eps = constants[:, 0:1], constants[:, 1:2]
        junk = [[silu[t].bitcast(BF16) for t in range(T)], [rope_tmp.bitcast(BF16)] * T]

        bank = [ctx.enter_context(nc.psum_tensor(f"bank{b}", [P, BANK], F32)) for b in range(8)]

        x_in_done = [sem(f"x_in_done{t}") for t in range(T)]
        tables_in = sem("tables_in")
        bias_in = sem("bias_in")
        sinks_loaded = sem("sinks_loaded")
        gain_a_in = sem("gain_a_in")
        gain_b_in = sem("gain_b_in")
        raw_in = [sem(f"raw_in{r}") for r in range(RAW)]
        raw_free = sem("raw_free")
        out_done = sem("out_done")
        const_ready = sem("const_ready")
        hi_ready = sem("hi_ready")
        lo_ready = sem("lo_ready")
        block_used = sem("block_used")
        full = [sem(f"full{b}") for b in range(8)]
        drained = [sem(f"drained{b}") for b in range(8)]
        hiT_ready = sem("hiT_ready")
        x_ready = sem("x_ready")
        rows_ready = sem("rows_ready")
        squares_x = sem("squares_x")
        rstd_x_ready = sem("rstd_x_ready")
        squares_y = sem("squares_y")
        rstd_y_ready = sem("rstd_y_ready")
        rotated = sem("rotated")
        max_ready = sem("max_ready")
        sink_arg_ready = sem("sink_arg_ready")
        sink_exp_ready = sem("sink_exp_ready")
        probsT_used = sem("probsT_used")
        o_ready = sem("o_ready")
        rstd_o_ready = sem("rstd_o_ready")
        o_scaled = sem("o_scaled")
        eps_added = sem("eps_added")
        pool_step = sem("pool_step")
        dve_step = sem("dve_step")

        HELD = [Order(names) for names in HOLDS]
        USED = Order([b for b in range(NB) if not completes(b, T - 1)])
        tiles = [(ph, t) for ph in range(2) for t in range(T)]
        X_READY, ROWS, SQ_X, R_X, R_Y = (Order(tiles) for _ in range(5))
        SQ_Y = Order([(ph, t, c) for ph, t in tiles for c in range(2)])
        groups = [(SWA, 0), (SWA, 1), (MOBA, 0), (MOBA, 1)]
        O_READY, R_O, O_SCALED = (Order(groups) for _ in range(3))
        ROTATED = Order([(0, 0), (1, 0), (0, 1), (1, 1), (2, 0), (2, 1), (3, 0), (3, 1)])
        rounds = [(g, r) for g in (SWA, MOBA) for r in range(3)]
        MAX = Order(rounds)
        PV = Order([(g, r, j) for g, r in rounds for j in range(2) if r == 1 or j == 0])
        SINK_ARG, SINK_EXP = Order([0, 1]), Order([0, 1])
        HIT = Order([("ht", 0, 0, 0), ("ht", 0, 0, 1), ("ht", 0, 1, 0), ("ht", 0, 1, 1), ("mix", SWA, 0),
                     ("mix", SWA, 1), ("mix", MOBA, 0), ("mix", MOBA, 1), ("ht", 1, 0, 0), ("ht", 1, 0, 1),
                     ("ht", 1, 1, 0), ("ht", 1, 1, 1)] + [("ft", c, t) for c in range(FFN_CHUNKS) for t in range(T)])

        def transposed(name):
            if name[0] == "ht":
                return actT, 4 * name[3], 4, name[2]
            if name[0] == "mix":
                return actT, 4 * name[1], 4, name[2]
            return fT, 4 * name[1], min(4, KF - 4 * name[1]), name[2]

        def tokens(t):
            return slice(t * P, (t + 1) * P)

        def broadcast(row, width):
            return row.rearrange("(a n) -> a n", a=1).broadcast_to([P, width])

        block = ctx.enter_context(nc.Block())

        @block.sync
        def _(sp):
            def load_block(L, b):
                m, k, nk, col, n = BLOCKS[b]
                sp.wait_ge(lo_ready, L * NB + b + 1)
                sp.sem_inc(raw_free, 1)
                sp.dma_start(raw[:, b % RAW, :].rearrange("p (k n) -> p k n", k=nk),
                             weights[m][L, k * P:(k + nk) * P, col:col + n].rearrange("(k p) n -> p k n", p=P)
                             ).then_inc(raw_in[b % RAW], 16)

            def load_layer_vectors(L):
                sp.dma_start(gain_a[:], broadcast(g_attn_pre[L], D)).then_inc(gain_a_in, 16)
                sp.dma_start(bias[:], broadcast(b_in[L], IN)).then_inc(bias_in, 16)
                sp.dma_start(sinks[:].rearrange("p j i -> p (j i)"), broadcast(sinks_in[L], HEADS)
                             ).then_inc(sinks_loaded, 16)

            sp.dma_start(x[:, 0, :], x_in[0, 0:P, :]).then_inc(x_in_done[0], 16)
            sp.dma_start(gain_a[:], broadcast(g_attn_pre[0], D)).then_inc(gain_a_in, 16)
            load_block(0, 0)
            sp.dma_start(x[:, 1, :], x_in[0, P:SEQ, :]).then_inc(x_in_done[1], 16)
            load_block(0, 1)
            sp.dma_start(cos[:], cos_in.rearrange("(t p) n -> p t n", p=P)).then_inc(tables_in, 16)
            sp.dma_start(sin[:], sin_in.rearrange("(t p) n -> p t n", p=P)).then_inc(tables_in, 16)
            sp.dma_start(bias[:], broadcast(b_in[0], IN)).then_inc(bias_in, 16)
            sp.dma_start(sinks[:].rearrange("p j i -> p (j i)"), broadcast(sinks_in[0], HEADS)
                         ).then_inc(sinks_loaded, 16)

            with sp.Fori(0, depth) as L:
                for b in range(2, NB):
                    load_block(L, b)
                    if b == 6:
                        sp.wait_ge(rows_ready, ROWS.done(L, (0, 1)))
                        sp.dma_start(gain_b[:], broadcast(g_attn_post[L], D)).then_inc(gain_b_in, 16)
                    if b == 8:
                        sp.wait_ge(rows_ready, ROWS.done(L, (0, 1)))
                        sp.dma_start(gain_a[:, 0:GROUP], broadcast(g_moba[L], GROUP)).then_inc(gain_a_in, 16)
                        sp.dma_start(gain_a[:, GROUP:D], broadcast(g_swa[L], GROUP)).then_inc(gain_a_in, 16)
                    if b == 12:
                        last = ("proj", 4, 1)
                        sp.wait_ge(drained[BANK_OF[last]], HELD[BANK_OF[last]].done(L, last) + 1)
                        sp.dma_start(gain_ffn, broadcast(g_ffn_pre[L], D)).then_inc(bias_in, 16)
                    if b == 24:
                        sp.wait_ge(x_ready, X_READY.done(L, (0, 1)))
                        sp.dma_start(gain_b[:], broadcast(g_ffn_post[L], D)).then_inc(gain_b_in, 16)
                with sp.If(L < depth - 1):
                    following = nc.s_assert_within(
                        L + 1, 1, depth - 1, skip_runtime_bounds_check_because="L < depth - 1 here")
                    sp.wait_ge(rows_ready, ROWS.done(L, (1, 1)))
                    load_layer_vectors(following)
                    load_block(following, 0)
                    load_block(following, 1)
            for t in range(T):
                sp.wait_ge(x_ready, X_READY.done(depth - 1, (1, t)))
                sp.dma_start(out[0, tokens(t), :], x[:, t, :]).then_inc(out_done, 16)
            sp.wait_ge(out_done, 16 * T)

        @block.gpsimd
        def _(pool):
            for b in range(8):
                pool.sem_inc(drained[b], 1)
            pool.sem_inc(block_used, USED.n)
            pool.sem_inc(lo_ready, RAW)
            nc.gpsimd.memset(ident[:], 0.0).then_inc(const_ready, 1)
            nc.gpsimd.memset(ident16[:], 0.0).then_inc(const_ready, 1)
            nc.gpsimd.memset(masks[:], 0.0).then_inc(const_ready, 1)
            nc.gpsimd.memset(minus_half, -0.5).then_inc(const_ready, 1)
            nc.gpsimd.memset(eps, EPS).then_inc(const_ready, 1)
            pool.wait_ge(const_ready, 5)
            for m in (ident, ident16):
                nc.gpsimd.affine_select(out=m[:], in_=m[:], compare_op=ALU.not_equal, fill=1.0, base=0,
                                        pattern=[[-1, P]], channel_multiplier=1).then_inc(const_ready, 1)
            for n in (1, 3):
                nc.gpsimd.affine_select(out=masks[:, n, :], in_=masks[:, n, :], compare_op=ALU.is_ge, fill=NEG,
                                        base=0, pattern=[[-1, P]], channel_multiplier=1).then_inc(const_ready, 1)
            nc.gpsimd.affine_select(out=masks[:, 2, :], in_=masks[:, 2, :], compare_op=ALU.is_gt, fill=NEG,
                                    base=0, pattern=[[1, P]], channel_multiplier=-1).then_inc(const_ready, 1)

            PER_LAYER = 20
            n_step = [0]

            def link(L, ins):
                n_step[0] += 1
                ins.then_inc(pool_step, 1)
                pool.wait_ge(pool_step, L * PER_LAYER + n_step[0])

            def rotate(L, ci, t):
                if ci == 0:
                    src = stage[t][:, 0:KV].rearrange("p (j i d) -> p j i d", j=2, i=1)
                    dst = roped[t][:, 0:KV].rearrange("p (i j d) -> p j i d", j=2, i=1)
                else:
                    src = stage[t].rearrange("p (j i d) -> p j i d", j=2, i=4)
                    dst = roped[t].rearrange("p (i j d) -> p j i d", j=2, i=4)
                n = src.shape[2]
                half = HEAD // 2
                c = cos[:, t, :].unsqueeze(1).unsqueeze(1).broadcast_to([P, 2, n, half])
                s = sin[:, t, :].unsqueeze(1).unsqueeze(1).broadcast_to([P, 2, n, half])
                tmp = [rope_tmp[:, q * 256:q * 256 + 2 * n * half].rearrange("p (j i d) -> p j i d", j=2, i=n)
                       for q in range(2)]
                x1, x2 = src[:, :, :, 0:half], src[:, :, :, half:HEAD]
                pool.wait_ge(drained[BANK_OF["proj", ci, t]],
                             HELD[BANK_OF["proj", ci, t]].done(L, ("proj", ci, t)) + 1)
                if ci:
                    b = BANK_OF["qk", ci - 1, t]
                    pool.wait_ge(full[b], HELD[b].done(L, ("qk", ci - 1, t)))
                if (ci, t) != ROTATED.names[0]:
                    pool.wait_ge(rotated, ROTATED.before(L, (ci, t)))
                nc.gpsimd.tensor_tensor(dst[:, :, :, 0:half], x1, c, ALU.mult)
                nc.gpsimd.tensor_tensor(tmp[0], x2, s, ALU.mult)
                nc.gpsimd.tensor_tensor(dst[:, :, :, half:HEAD], x2, c, ALU.mult)
                link(L, nc.gpsimd.tensor_tensor(tmp[1], x1, s, ALU.mult))
                nc.gpsimd.tensor_tensor(dst[:, :, :, 0:half], dst[:, :, :, 0:half], tmp[0], ALU.subtract)
                nc.gpsimd.tensor_tensor(dst[:, :, :, half:HEAD], dst[:, :, :, half:HEAD], tmp[1], ALU.add
                                        ).then_inc(rotated, 1)
                ROTATED.tick((ci, t))

            def one_over_rms(L, mean_square, rstd, ready):
                link(L, nc.gpsimd.tensor_tensor(mean_square, mean_square, eps, ALU.add))
                nc.gpsimd.tensor_tensor(rstd, mean_square, minus_half, ALU.pow).then_inc(ready, 1)

            def rms_x(L, ph, t):
                pool.wait_ge(squares_x, SQ_X.done(L, (ph, t)))
                nc.gpsimd.tensor_tensor(ss_x[:, t:t + 1], ss_x[:, t:t + 1], eps, ALU.add).then_inc(eps_added, 1)
                pool.wait_ge(eps_added, R_X.done(L, (ph, t)))
                nc.gpsimd.tensor_tensor(rstd_x[:, t:t + 1], ss_x[:, t:t + 1], minus_half, ALU.pow
                                        ).then_inc(rstd_x_ready, 1)
                R_X.tick((ph, t))

            def rms_y(L, ph, t):
                pool.wait_ge(squares_y, SQ_Y.done(L, (ph, t, 1)))
                link(L, nc.gpsimd.tensor_tensor(ss_y[:, t, 0:1], ss_y[:, t, 0:1], ss_y[:, t, 1:2], ALU.add))
                one_over_rms(L, ss_y[:, t, 0:1], rstd_y[:, t:t + 1], rstd_y_ready)
                R_Y.tick((ph, t))

            def rms_o(L, g, t):
                b = BANK_OF["pv", g, t]
                pool.wait_ge(drained[b], HELD[b].done(L, ("pv", g, t)) + 1)
                one_over_rms(L, ss_o[:, t:t + 1], rstd_o[:, t:t + 1], rstd_o_ready)
                R_O.tick((g, t))

            pool.wait_ge(const_ready, 10)
            pool.wait_ge(tables_in, 32)
            for t in range(T):
                rms_x(0, 0, t)
            with pool.Fori(0, depth) as L:
                rotate(L, 0, 0)
                rotate(L, 1, 0)
                rotate(L, 0, 1)
                rotate(L, 1, 1)
                rotate(L, 2, 0)
                rotate(L, 2, 1)
                rms_o(L, SWA, 0)
                rotate(L, 3, 0)
                rotate(L, 3, 1)
                rms_o(L, SWA, 1)
                rms_o(L, MOBA, 0)
                rms_y(L, 0, 0)
                rms_x(L, 1, 0)
                rms_o(L, MOBA, 1)
                rms_y(L, 0, 1)
                rms_x(L, 1, 1)
                rms_y(L, 1, 0)
                with pool.If(L < depth - 1):
                    rms_x(L + 1, 0, 0)
                rms_y(L, 1, 1)
                with pool.If(L < depth - 1):
                    rms_x(L + 1, 0, 1)
                assert n_step[0] == PER_LAYER, n_step

        @block.scalar
        def _(act):
            def hi(L, b):
                act.wait_ge(raw_in[b % RAW], (L * (NB // RAW) + b // RAW + 1) * 16)
                last = before(b)
                if last < 0 and completes(last % NB, T - 1):
                    pass
                elif completes(last % NB, T - 1):
                    name = completes(last, T - 1)[-1]
                    act.wait_ge(full[BANK_OF[name]], HELD[BANK_OF[name]].done(L, name))
                else:
                    act.wait_ge(block_used, USED.done(L, last % NB) + (USED.n if last >= 0 else 0))
                nc.scalar.activation(w["h"][:, slot(b), :], raw[:, b % RAW, :], ACT.Copy).then_inc(hi_ready, 1)

            def after(L, b):
                for c in freed_by(b):
                    if c < NB:
                        hi(L, c)

            def hiT(L, name):
                b = BANK_OF[name]
                dst, k, nk, t = transposed(name)
                act.wait_ge(full[b], HELD[b].done(L, name))
                nc.scalar.activation(dst["h"][:, k:k + nk, tokens(t)],
                                     bank[b][:, 0:nk * P].rearrange("p (k n) -> p k n", k=nk), ACT.Copy
                                     ).then_inc(hiT_ready, 1)
                HIT.tick(name)

            def sum_x(L, ph, t):
                nc.scalar.activation(junk[ph][t], x[:, t, :], ACT.Square, scale=D ** -0.5,
                                     accum_out=ss_x[:, t:t + 1]).then_inc(squares_x, 1)
                SQ_X.tick((ph, t))

            def sum_y(L, ph, t):
                for c in range(2):
                    name = ("down" if ph else "out", t, c)
                    b = BANK_OF[name]
                    act.wait_ge(full[b], HELD[b].done(L, name))
                    nc.scalar.activation(y[t][:, c, :], bank[b][:], ACT.Square, scale=D ** -0.5,
                                         accum_out=ss_y[:, t, c:c + 1]).then_inc(squares_y, 1)
                    SQ_Y.tick((ph, t, c))

            def keep_qk(L, ci, t):
                b = BANK_OF["qk", ci, t]
                act.wait_ge(full[b], HELD[b].done(L, ("qk", ci, t)))
                dst = (kT[SWA], qT[SWA], kT[MOBA], qT[MOBA])[ci]
                n = dst.shape[1]
                nc.scalar.activation(dst[:, :, tokens(t)], bank[b][:, 0:n * P].rearrange("p (i n) -> p i n", i=n),
                                     ACT.Copy).then_inc(drained[b], 1)

            def exps(L, g, r, earlier=None):
                t, pairs = ROUNDS[r]
                keys = P * (t + 1)
                act.wait_ge(max_ready, MAX.done(L, (g, r)))
                for j in range(2):
                    if (g, r) != (SWA, 0):
                        pg, pr = rounds[rounds.index((g, r)) - 1]
                        act.wait_ge(full[6], HELD[6].done(L, ("pt", pg, pr, j)))
                    for n, i in enumerate(pairs):
                        last = nc.scalar.activation(probs[:, j, n * keys:(n + 1) * keys],
                                                    bank[4 + j][:, n * keys:(n + 1) * keys], ACT.Exp,
                                                    bias=neg_max[:, g, t, j, i:i + 1], scale=SCALE,
                                                    accum_out=row_sum[:, g, t, j, i:i + 1])
                    last.then_inc(drained[4 + j], 1)

            def sink_exps(L, t):
                act.wait_ge(sink_arg_ready, SINK_ARG.done(L, t))
                nc.scalar.activation(sink_exp[:], sink_exp[:], ACT.Exp).then_inc(sink_exp_ready, 1)
                SINK_EXP.tick(t)

            def sum_o(L, g, t):
                b = BANK_OF["pv", g, t]
                act.wait_ge(o_ready, O_READY.done(L, (g, t)))
                nc.scalar.activation(bank[b][:], o[t], ACT.Square, scale=GROUP ** -0.5, accum_out=ss_o[:, t:t + 1]
                                     ).then_inc(drained[b], 1)

            def silus(L, c, t):
                n = min(BANK, FF - c * BANK)
                b = BANK_OF["gate", c, t]
                act.wait_ge(full[b], HELD[b].done(L, ("gate", c, t)))
                if c == 0:
                    act.wait_ge(rstd_x_ready, R_X.done(L, (1, t)))
                else:
                    bu = BANK_OF["up", c - 1, t]
                    act.wait_ge(drained[bu], HELD[bu].done(L, ("up", c - 1, t)) + 1)
                nc.scalar.activation(silu[t][:, 0:n], bank[b][:, 0:n], ACT.Silu, scale=rstd_x[:, t:t + 1]
                                     ).then_inc(drained[b], 1)

            hi(0, 0)
            act.wait_ge(x_in_done[0], 16)
            sum_x(0, 0, 0)
            hi(0, 1)
            act.wait_ge(x_in_done[1], 16)
            sum_x(0, 0, 1)
            hi(0, 2)
            with act.Fori(0, depth) as L:
                hiT(L, ("ht", 0, 0, 0))
                hiT(L, ("ht", 0, 0, 1))
                hi(L, 3)
                hiT(L, ("ht", 0, 1, 0))
                hiT(L, ("ht", 0, 1, 1))
                keep_qk(L, 0, 0)
                after(L, 0)
                keep_qk(L, 1, 0)
                after(L, 1)
                keep_qk(L, 0, 1)
                after(L, 2)
                exps(L, SWA, 0)
                sink_exps(L, 0)
                keep_qk(L, 1, 1)
                after(L, 3)
                after(L, 4)
                exps(L, SWA, 1)
                sum_o(L, SWA, 0)
                keep_qk(L, 2, 0)
                after(L, 5)
                exps(L, SWA, 2)
                sink_exps(L, 1)
                keep_qk(L, 2, 1)
                after(L, 6)
                keep_qk(L, 3, 0)
                exps(L, MOBA, 0)
                after(L, 7)
                keep_qk(L, 3, 1)
                after(L, 8)
                hiT(L, ("mix", SWA, 0))
                sum_o(L, SWA, 1)
                hiT(L, ("mix", SWA, 1))
                exps(L, MOBA, 1)
                sum_o(L, MOBA, 0)
                after(L, 9)
                after(L, 10)
                hiT(L, ("mix", MOBA, 0))
                exps(L, MOBA, 2)
                sum_y(L, 0, 0)
                sum_o(L, MOBA, 1)
                act.wait_ge(x_ready, X_READY.done(L, (0, 0)))
                sum_x(L, 1, 0)
                hiT(L, ("mix", MOBA, 1))
                after(L, 11)
                hiT(L, ("ht", 1, 0, 0))
                hiT(L, ("ht", 1, 0, 1))
                after(L, 12)
                sum_y(L, 0, 1)
                act.wait_ge(x_ready, X_READY.done(L, (0, 1)))
                sum_x(L, 1, 1)
                hiT(L, ("ht", 1, 1, 0))
                hiT(L, ("ht", 1, 1, 1))
                silus(L, 0, 0)
                after(L, 13)
                after(L, 14)
                silus(L, 0, 1)
                after(L, 15)
                after(L, 16)
                for c in range(1, FFN_CHUNKS):
                    b = FIRST_FFN + 4 * c
                    hiT(L, ("ft", c - 1, 0))
                    after(L, b)
                    hiT(L, ("ft", c - 1, 1))
                    silus(L, c, 0)
                    silus(L, c, 1)
                    for q in range(1, 2 if c == FFN_CHUNKS - 1 else 4):
                        after(L, b + q)
                hiT(L, ("ft", FFN_CHUNKS - 1, 0))
                after(L, FIRST_DOWN)
                hiT(L, ("ft", FFN_CHUNKS - 1, 1))
                for b in range(FIRST_DOWN + 1, NB - 4):
                    after(L, b)
                sum_y(L, 1, 0)
                with act.If(L < depth - 1):
                    hi(L + 1, 0)
                    act.wait_ge(x_ready, X_READY.done(L, (1, 0)))
                    sum_x(L + 1, 0, 0)
                    hi(L + 1, 1)
                    hi(L + 1, 2)
                sum_y(L, 1, 1)
                with act.If(L < depth - 1):
                    act.wait_ge(x_ready, X_READY.done(L, (1, 1)))
                    sum_x(L + 1, 0, 1)

        @block.vector
        def _(dve):
            PER_LAYER = 15
            n_step = [0]

            def link(L, ins):
                n_step[0] += 1
                ins.then_inc(dve_step, 1)
                dve.wait_ge(dve_step, L * PER_LAYER + n_step[0])

            def lo(L, b):
                dve.wait_ge(hi_ready, L * NB + b + 1)
                nc.vector.tensor_tensor(w["l"][:, slot(b), :], raw[:, b % RAW, :],
                                        w["h"][:, slot(b), :].bitcast(F32), ALU.subtract).then_inc(lo_ready, 1)

            def after(L, b):
                for c in freed_by(b):
                    if c < NB:
                        lo(L, c)

            def loT(L, name):
                b = BANK_OF[name]
                dst, k, nk, t = transposed(name)
                dve.wait_ge(hiT_ready, HIT.done(L, name))
                nc.vector.tensor_tensor(dst["l"][:, k:k + nk, tokens(t)],
                                        bank[b][:, 0:nk * P].rearrange("p (k n) -> p k n", k=nk),
                                        dst["h"][:, k:k + nk, tokens(t)].bitcast(F32), ALU.subtract
                                        ).then_inc(drained[b], 1)

            def scale_rows(L, ph, t):
                if ph == 0:
                    dve.wait_ge(gain_a_in, (L * 3 + 1) * 16)
                else:
                    dve.wait_ge(bias_in, (L * 2 + 2) * 16)
                gain = gain_ffn if ph else gain_a[:]
                nc.vector.tensor_tensor(y[t].rearrange("p a n -> p (a n)"), x[:, t, :], gain, ALU.mult
                                        ).then_inc(rows_ready, 1)
                ROWS.tick((ph, t))

            def project(L, ci, t):
                b = BANK_OF["proj", ci, t]
                col, n = PROJ_COLS[ci]
                if (ci, t) == (0, 0):
                    dve.wait_ge(bias_in, (L * 2 + 1) * 16)
                if ci == 0:
                    dve.wait_ge(rstd_x_ready, R_X.done(L, (0, t)))
                dve.wait_ge(full[b], HELD[b].done(L, ("proj", ci, t)))
                if 0 < ci < 4:
                    dve.wait_ge(rotated, ROTATED.done(L, (ci - 1, t)))
                dst = v[MOBA][:, t, :] if ci == 4 else stage[t][:, 0:n]
                if ci == 0:
                    n = KV
                    nc.vector.scalar_tensor_tensor(v[SWA][:, t, :], bank[b][:, KV:2 * KV], rstd_x[:, t:t + 1],
                                                   bias[:, col + KV:col + 2 * KV], ALU.mult, ALU.add)
                nc.vector.scalar_tensor_tensor(dst[:, 0:n], bank[b][:, 0:n], rstd_x[:, t:t + 1],
                                               bias[:, col:col + n], ALU.mult, ALU.add).then_inc(drained[b], 1)

            def maxima(L, g, r):
                t, pairs = ROUNDS[r]
                n = len(pairs)
                i = slice(pairs[0], pairs[0] + n)
                for j in range(2):
                    dve.wait_ge(full[4 + j], HELD[4 + j].done(L, ("scores", g, r, j)))
                    ins = nc.vector.tensor_reduce(top[:, j, i], bank[4 + j][:].rearrange("p (i n) -> p i n", i=n),
                                                  AX.X, ALU.max)
                link(L, ins)
                if g == SWA:
                    if r == 0:
                        dve.wait_ge(sinks_loaded, (L + 1) * 16)
                    link(L, nc.vector.scalar_tensor_tensor(top[:, :, i], top[:, :, i], SCALE, sinks[:, :, i],
                                                           ALU.mult, ALU.max))
                    ins = nc.vector.tensor_scalar(neg_max[:, g, t, :, i], top[:, :, i], -1.0, None, ALU.mult)
                else:
                    ins = nc.vector.tensor_scalar(neg_max[:, g, t, :, i], top[:, :, i], -SCALE, None, ALU.mult)
                ins.then_inc(max_ready, 1)
                MAX.tick((g, r))
                if g == SWA and r != 1:
                    dve.wait_ge(max_ready, MAX.done(L, (g, r)))
                    nc.vector.tensor_tensor(sink_exp[:], sinks[:], neg_max[:, g, t, :, :], ALU.add
                                            ).then_inc(sink_arg_ready, 1)
                    SINK_ARG.tick(t)

            def keep_probsT(L, g, r, j):
                dve.wait_ge(full[6], HELD[6].done(L, ("pt", g, r, j)))
                if (g, r) != (SWA, 0):
                    pg, pr = rounds[rounds.index((g, r)) - 1]
                    if j == 1 and pr != 1:
                        dve.wait_ge(full[7], HELD[7].done(L, ("pv", pg, ROUNDS[pr][0])))
                    else:
                        dve.wait_ge(probsT_used, PV.done(L, (pg, pr, j)))
                nc.vector.tensor_copy(probsT[:, j, :], bank[6][:]).then_inc(drained[6], 1)

            def normalise(L, g, t):
                b = BANK_OF["pv", g, t]
                sums = row_sum[:, g, t, :, :].rearrange("p j i -> p (j i)")
                dve.wait_ge(full[b], HELD[b].done(L, ("pv", g, t)))
                if g == SWA:
                    dve.wait_ge(sink_exp_ready, SINK_EXP.done(L, t))
                    link(L, nc.vector.tensor_tensor(sums, sums, sink_exp[:].rearrange("p j i -> p (j i)"), ALU.add))
                link(L, nc.vector.reciprocal(sums, sums))
                nc.vector.tensor_tensor(o[t].rearrange("p (h d) -> p h d", h=HEADS),
                                        bank[b][:].rearrange("p (h d) -> p h d", h=HEADS),
                                        sums.unsqueeze(2).broadcast_to([P, HEADS, HEAD]), ALU.mult
                                        ).then_inc(o_ready, 1)
                O_READY.tick((g, t))

            def scale_o(L, g, t):
                if (g, t) == (SWA, 0):
                    dve.wait_ge(gain_a_in, (L * 3 + 3) * 16)
                dve.wait_ge(rstd_o_ready, R_O.done(L, (g, t)))
                nc.vector.scalar_tensor_tensor(o[t], o[t], rstd_o[:, t:t + 1], gain_a[:, g * GROUP:(g + 1) * GROUP],
                                               ALU.mult, ALU.mult).then_inc(o_scaled, 1)
                O_SCALED.tick((g, t))

            def scale_y(L, ph, t):
                for c in range(2):
                    name = ("down" if ph else "out", t, c)
                    b = BANK_OF[name]
                    if (t, c) == (0, 0):
                        dve.wait_ge(gain_b_in, (L * 2 + ph + 1) * 16)
                    dve.wait_ge(squares_y, SQ_Y.done(L, (ph, t, c)))
                    nc.vector.tensor_tensor(y[t][:, c, :], bank[b][:], gain_b[:, c * BANK:(c + 1) * BANK], ALU.mult
                                            ).then_inc(drained[b], 1)

            def update_x(L, ph, t):
                b = BANK_OF["down" if ph else "out", t, 1]
                dve.wait_ge(drained[b], HELD[b].done(L, ("down" if ph else "out", t, 1)) + 1)
                dve.wait_ge(rstd_y_ready, R_Y.done(L, (ph, t)))
                nc.vector.scalar_tensor_tensor(x[:, t, :], y[t].rearrange("p a n -> p (a n)"), rstd_y[:, t:t + 1],
                                               x[:, t, :], ALU.mult, ALU.add).then_inc(x_ready, 1)
                X_READY.tick((ph, t))

            def swiglu(L, c, t):
                n = min(BANK, FF - c * BANK)
                b = BANK_OF["up", c, t]
                dve.wait_ge(full[b], HELD[b].done(L, ("up", c, t)))
                bg = BANK_OF["gate", c, t]
                dve.wait_ge(drained[bg], HELD[bg].done(L, ("gate", c, t)) + 1)
                if c:
                    bt = BANK_OF["ft", c - 1, t]
                    dve.wait_ge(full[bt], HELD[bt].done(L, ("ft", c - 1, t)))
                nc.vector.scalar_tensor_tensor(f[t][:, 0:n], bank[b][:, 0:n], rstd_x[:, t:t + 1], silu[t][:, 0:n],
                                               ALU.mult, ALU.mult).then_inc(drained[b], 1)

            for t in range(T):
                dve.wait_ge(x_in_done[t], 16)
                scale_rows(0, 0, t)
            lo(0, 0)
            lo(0, 1)
            lo(0, 2)
            with dve.Fori(0, depth) as L:
                loT(L, ("ht", 0, 0, 0))
                loT(L, ("ht", 0, 0, 1))
                lo(L, 3)
                project(L, 0, 0)
                loT(L, ("ht", 0, 1, 0))
                loT(L, ("ht", 0, 1, 1))
                project(L, 1, 0)
                project(L, 0, 1)
                after(L, 0)
                after(L, 1)
                project(L, 1, 1)
                after(L, 2)
                maxima(L, SWA, 0)
                project(L, 2, 0)
                after(L, 3)
                keep_probsT(L, SWA, 0, 0)
                project(L, 2, 1)
                keep_probsT(L, SWA, 0, 1)
                after(L, 4)
                maxima(L, SWA, 1)
                normalise(L, SWA, 0)
                keep_probsT(L, SWA, 1, 0)
                project(L, 3, 0)
                scale_o(L, SWA, 0)
                after(L, 5)
                keep_probsT(L, SWA, 1, 1)
                maxima(L, SWA, 2)
                project(L, 3, 1)
                after(L, 6)
                keep_probsT(L, SWA, 2, 0)
                project(L, 4, 0)
                maxima(L, MOBA, 0)
                keep_probsT(L, SWA, 2, 1)
                after(L, 7)
                normalise(L, SWA, 1)
                project(L, 4, 1)
                after(L, 8)
                loT(L, ("mix", SWA, 0))
                scale_o(L, SWA, 1)
                keep_probsT(L, MOBA, 0, 0)
                loT(L, ("mix", SWA, 1))
                keep_probsT(L, MOBA, 0, 1)
                maxima(L, MOBA, 1)
                normalise(L, MOBA, 0)
                after(L, 9)
                scale_o(L, MOBA, 0)
                keep_probsT(L, MOBA, 1, 0)
                after(L, 10)
                loT(L, ("mix", MOBA, 0))
                keep_probsT(L, MOBA, 1, 1)
                maxima(L, MOBA, 2)
                keep_probsT(L, MOBA, 2, 0)
                keep_probsT(L, MOBA, 2, 1)
                scale_y(L, 0, 0)
                normalise(L, MOBA, 1)
                update_x(L, 0, 0)
                scale_o(L, MOBA, 1)
                loT(L, ("mix", MOBA, 1))
                dve.wait_ge(x_ready, X_READY.done(L, (0, 0)))
                scale_rows(L, 1, 0)
                after(L, 11)
                loT(L, ("ht", 1, 0, 0))
                loT(L, ("ht", 1, 0, 1))
                after(L, 12)
                scale_y(L, 0, 1)
                update_x(L, 0, 1)
                dve.wait_ge(x_ready, X_READY.done(L, (0, 1)))
                scale_rows(L, 1, 1)
                loT(L, ("ht", 1, 1, 0))
                loT(L, ("ht", 1, 1, 1))
                after(L, 13)
                after(L, 14)
                swiglu(L, 0, 0)
                after(L, 15)
                after(L, 16)
                swiglu(L, 0, 1)
                for c in range(1, FFN_CHUNKS):
                    b = FIRST_FFN + 4 * c
                    end = b + (1 if c == FFN_CHUNKS - 1 else 3)
                    loT(L, ("ft", c - 1, 0))
                    after(L, b)
                    loT(L, ("ft", c - 1, 1))
                    for q in range(b + 1, end):
                        after(L, q)
                    swiglu(L, c, 0)
                    after(L, end)
                    swiglu(L, c, 1)
                loT(L, ("ft", FFN_CHUNKS - 1, 0))
                after(L, FIRST_DOWN)
                loT(L, ("ft", FFN_CHUNKS - 1, 1))
                for b in range(FIRST_DOWN + 1, NB - 4):
                    after(L, b)
                scale_y(L, 1, 0)
                with dve.If(L < depth - 1):
                    lo(L + 1, 0)
                update_x(L, 1, 0)
                with dve.If(L < depth - 1):
                    dve.wait_ge(x_ready, X_READY.done(L, (1, 0)))
                    scale_rows(L + 1, 0, 0)
                    lo(L + 1, 1)
                    lo(L + 1, 2)
                scale_y(L, 1, 1)
                update_x(L, 1, 1)
                with dve.If(L < depth - 1):
                    dve.wait_ge(x_ready, X_READY.done(L, (1, 1)))
                    scale_rows(L + 1, 0, 1)
                assert n_step[0] == PER_LAYER, n_step

        @block.tensor
        def _(pe):
            def claim(L, name):
                b = BANK_OF[name]
                HELD[b].tick(name)
                pe.wait_ge(drained[b], HELD[b].before(L, name) + 1)
                return bank[b]

            def landed(L, name):
                b = BANK_OF[name]
                pe.wait_ge(drained[b], HELD[b].done(L, name) + 1)

            def multiply(L, t, b):
                m, k0, nk, col, n = BLOCKS[b]
                first = k0 == (4 if m == "out" else 0)
                final = completes(b, t)
                if m == "in":
                    names = [("proj", (b + 1) // 2, t)]
                elif m == "down":
                    names = [("down", t, c) for c in range(2)]
                elif m == "out":
                    names = [("out", t, col // BANK)]
                else:
                    names = [(m, col // BANK, t)]
                if t == 0:
                    pe.wait_ge(lo_ready, L * NB + b + 1 + RAW)
                if first:
                    for name in names:
                        claim(L, name)
                left = fT if m == "down" else actT
                n = min(n, BANK)
                right = {s: w[s][:, slot(b), :].rearrange("p (k n) -> p k n", k=nk) for s in "hl"}
                for k in range(nk):
                    for s, r in (("h", "h"), ("h", "l"), ("l", "h")):
                        for c, name in enumerate(names):
                            ins = nc.tensor.matmul(bank[BANK_OF[name]][:, 0:n], left[s][:, k0 + k, tokens(t)],
                                                   right[r][:, k, c * BANK:c * BANK + n],
                                                   start=first and k == 0 and (s, r) == ("h", "h"),
                                                   stop=name in final and k == nk - 1 and (s, r) == ("l", "h"))
                            if name in final and k == nk - 1 and (s, r) == ("l", "h"):
                                ins.then_inc(full[BANK_OF[name]], 1)
                if t == T - 1 and not final:
                    ins.then_inc(block_used, 1)
                    USED.tick(b)

            def transpose(L, name, src, n):
                out_ = claim(L, name)
                for q in range(n):
                    ins = nc.tensor.transpose(out_[:, q * P:(q + 1) * P], src(q), ident[:])
                ins.then_inc(full[BANK_OF[name]], 1)

            def rows(L, ph, t):
                pe.wait_ge(rows_ready, ROWS.done(L, (ph, t)))
                for half in range(2):
                    transpose(L, ("ht", ph, t, half), lambda q: y[t][:, half, q * P:(q + 1) * P], 4)

            def qk(L, ci, t):
                pe.wait_ge(rotated, ROTATED.done(L, (ci, t)))
                transpose(L, ("qk", ci, t), lambda q: roped[t][:, q * P:(q + 1) * P], 1 if ci == 0 else 4)

            def scores(L, g, r):
                t, pairs = ROUNDS[r]
                keys = P * (t + 1)
                last_q, last_k = (("qk", 1, t), ("qk", 0, t)) if g == SWA else (("qk", 3, t), ("qk", 2, t))
                for name in (last_q, last_k):
                    landed(L, name)
                for j in range(2):
                    out_ = claim(L, ("scores", g, r, j))
                    if t == 0:
                        mask = masks[:, 1:2, :]
                    elif g == MOBA:
                        mask = masks[:, 0:2, :]
                    else:
                        mask = masks[:, 2:4, :]
                    mask = mask.rearrange("p a n -> p (a n)").unsqueeze(1).broadcast_to([P, len(pairs), keys])
                    nc.tensor.matmul(out_[:].rearrange("p (i n) -> p i n", i=len(pairs)), ident16[:], mask,
                                     start=True, stop=False)
                for n, i in enumerate(pairs):
                    for j in range(2):
                        side = slice(j * HEAD, (j + 1) * HEAD)
                        last = n == len(pairs) - 1
                        ins = nc.tensor.matmul(bank[4 + j][:, n * keys:(n + 1) * keys], qT[g][side, i, tokens(t)],
                                               kT[g][side, i if g == MOBA else 0, 0:keys], start=False, stop=last)
                        if last:
                            ins.then_inc(full[4 + j], 1)

            def probs_transposed(L, g, r, j):
                pe.wait_ge(drained[4 + j], HELD[4 + j].done(L, ("scores", g, r, j)) + 1)
                transpose(L, ("pt", g, r, j), lambda q: probs[:, j, q * P:(q + 1) * P], 4)

            def values(L, g, r, j):
                t, pairs = ROUNDS[r]
                if r < 2 and j == 0:
                    claim(L, ("pv", g, t))
                landed(L, ("pt", g, r, j))
                b = BANK_OF["pv", g, t]
                blocks = t + 1
                if j == 0:
                    ci = 0 if g == SWA else 4
                    landed(L, ("proj", ci, t))
                for n, i in enumerate(pairs):
                    h = 4 * j + i
                    cols = slice(h * HEAD, (h + 1) * HEAD) if g == MOBA else slice(j * HEAD, (j + 1) * HEAD)
                    for kb in range(blocks):
                        at = (n * blocks + kb) * P
                        ins = nc.tensor.matmul(bank[b][:, h * HEAD:(h + 1) * HEAD], probsT[:, j, at:at + P],
                                               v[g][:, kb, cols], start=kb == 0, stop=kb == blocks - 1)
                if j == 1 and r != 1:
                    ins.then_inc(full[b], 1)
                else:
                    ins.then_inc(probsT_used, 1)
                    PV.tick((g, r, j))

            def mix(L, g, t):
                pe.wait_ge(o_scaled, O_SCALED.done(L, (g, t)))
                transpose(L, ("mix", g, t), lambda q: o[t][:, q * P:(q + 1) * P], 4)

            def f_transposed(L, c, t):
                b = BANK_OF["up", c, t]
                pe.wait_ge(drained[b], HELD[b].done(L, ("up", c, t)) + 1)
                transpose(L, ("ft", c, t), lambda q: f[t][:, q * P:(q + 1) * P], min(4, KF - 4 * c))

            def rows_landed(L, ph, t):
                for half in range(2):
                    landed(L, ("ht", ph, t, half))

            pe.wait_ge(const_ready, 10)
            rows(0, 0, 0)
            with pe.Fori(0, depth) as L:
                rows_landed(L, 0, 0)
                multiply(L, 0, 0)
                rows(L, 0, 1)
                multiply(L, 0, 1)
                multiply(L, 0, 2)
                qk(L, 0, 0)
                rows_landed(L, 0, 1)
                multiply(L, 1, 0)
                multiply(L, 1, 1)
                qk(L, 1, 0)
                multiply(L, 1, 2)
                qk(L, 0, 1)
                multiply(L, 0, 3)
                scores(L, SWA, 0)
                multiply(L, 0, 4)
                qk(L, 1, 1)
                multiply(L, 1, 3)
                probs_transposed(L, SWA, 0, 0)
                multiply(L, 1, 4)
                probs_transposed(L, SWA, 0, 1)
                values(L, SWA, 0, 0)
                scores(L, SWA, 1)
                multiply(L, 0, 5)
                values(L, SWA, 0, 1)
                qk(L, 2, 0)
                multiply(L, 0, 6)
                probs_transposed(L, SWA, 1, 0)
                multiply(L, 1, 5)
                probs_transposed(L, SWA, 1, 1)
                values(L, SWA, 1, 0)
                scores(L, SWA, 2)
                multiply(L, 1, 6)
                values(L, SWA, 1, 1)
                qk(L, 2, 1)
                multiply(L, 0, 7)
                qk(L, 3, 0)
                multiply(L, 0, 8)
                probs_transposed(L, SWA, 2, 0)
                scores(L, MOBA, 0)
                multiply(L, 1, 7)
                probs_transposed(L, SWA, 2, 1)
                values(L, SWA, 2, 0)
                multiply(L, 1, 8)
                values(L, SWA, 2, 1)
                qk(L, 3, 1)
                mix(L, SWA, 0)
                landed(L, ("mix", SWA, 0))
                multiply(L, 0, 9)
                probs_transposed(L, MOBA, 0, 0)
                multiply(L, 0, 10)
                mix(L, SWA, 1)
                probs_transposed(L, MOBA, 0, 1)
                values(L, MOBA, 0, 0)
                scores(L, MOBA, 1)
                multiply(L, 1, 9)
                values(L, MOBA, 0, 1)
                multiply(L, 1, 10)
                probs_transposed(L, MOBA, 1, 0)
                mix(L, MOBA, 0)
                landed(L, ("mix", MOBA, 0))
                multiply(L, 0, 11)
                probs_transposed(L, MOBA, 1, 1)
                values(L, MOBA, 1, 0)
                scores(L, MOBA, 2)
                multiply(L, 0, 12)
                values(L, MOBA, 1, 1)
                probs_transposed(L, MOBA, 2, 0)
                probs_transposed(L, MOBA, 2, 1)
                values(L, MOBA, 2, 0)
                values(L, MOBA, 2, 1)
                mix(L, MOBA, 1)
                landed(L, ("mix", MOBA, 1))
                multiply(L, 1, 11)
                rows(L, 1, 0)
                multiply(L, 1, 12)
                rows_landed(L, 1, 0)
                b = FIRST_FFN
                multiply(L, 0, b)
                multiply(L, 0, b + 1)
                multiply(L, 0, b + 2)
                rows(L, 1, 1)
                multiply(L, 0, b + 3)
                rows_landed(L, 1, 1)
                multiply(L, 1, b)
                multiply(L, 1, b + 1)
                multiply(L, 1, b + 2)
                multiply(L, 1, b + 3)
                for c in range(1, FFN_CHUNKS):
                    b = FIRST_FFN + 4 * c
                    multiply(L, 0, b)
                    f_transposed(L, c - 1, 0)
                    multiply(L, 1, b)
                    f_transposed(L, c - 1, 1)
                    for q in range(1, 2 if c == FFN_CHUNKS - 1 else 4):
                        multiply(L, 0, b + q)
                        multiply(L, 1, b + q)
                for t in range(T):
                    landed(L, ("ft", FFN_CHUNKS - 2, t))
                for b in range(FIRST_DOWN, NB - 4):
                    multiply(L, 0, b)
                    if b == FIRST_DOWN:
                        f_transposed(L, FFN_CHUNKS - 1, 0)
                    multiply(L, 1, b)
                    if b == FIRST_DOWN:
                        f_transposed(L, FFN_CHUNKS - 1, 1)
                for t in range(T):
                    landed(L, ("ft", FFN_CHUNKS - 1, t))
                for b in range(NB - 4, NB):
                    multiply(L, 0, b)
                for b in range(NB - 4, NB):
                    if b == NB - 1:
                        with pe.If(L < depth - 1):
                            rows(L + 1, 0, 0)
                    multiply(L, 1, b)


def kernel(**inputs):
    import numpy as np
    import concourse.bacc as bacc
    from concourse.bass_utils import run_bass_kernel_spmd as run

    nc = bacc.Bacc("TRN2", target_bir_lowering=False, num_devices=1)
    names = ["x", "w_in", "b_in", "w_out", "g_attn_pre", "g_attn_post", "g_moba_out", "g_swa_out",
             "attn_sinks", "g_ffn_pre", "g_ffn_post", "w_gate", "w_up", "w_down"]
    arrays = {n: np.ascontiguousarray(inputs[n]) for n in names}
    steps = np.arange(0, HEAD, 2, dtype=np.float32) / np.float32(HEAD)
    inverse = np.float32(1.0) / np.float32(10000.0) ** steps
    angle = np.arange(SEQ, dtype=np.float32)[:, None] * inverse[None, :]
    arrays["rope_cos"] = np.cos(angle)
    arrays["rope_sin"] = np.sin(angle)
    args = [nc.dram_tensor("in_" + n, a.shape, mybir.dt.from_np(a.dtype), kind="ExternalInput").ap()
            for n, a in arrays.items()]
    args.append(nc.dram_tensor("out", (1, SEQ, D), F32, kind="ExternalOutput").ap())
    trunk(nc, *args)
    got = run(nc, [{"in_" + n: a for n, a in arrays.items()}], core_ids=[0])
    return got.results[0]["out"]
```

```python
from contextlib import ExitStack

import concourse.bass as bass
from concourse import mybir

F32 = mybir.dt.float32
F32R = mybir.dt.float32r
BF16 = mybir.dt.bfloat16
ACT = mybir.ActivationFunctionType
ALU = mybir.AluOpType
AX = mybir.AxisListType

P = 128
D = 1024
T = 2
SEQ = P * T
HEAD = 64
HEADS = 8
GROUP = HEADS * HEAD
KV = 2 * HEAD
IN = 4 * GROUP + 2 * KV
FF = 2816
BANK = 512
SCALE = HEAD ** -0.5
EPS = 1e-6
NEG = -1e30
MOBA, SWA = 0, 1

BLOCK = 2048
BLOCKS = [("in", 0, 8, 3 * GROUP + GROUP, 256)]
for col in (3 * GROUP, GROUP, 0, 2 * GROUP):
    BLOCKS += [("in", k, 4, col, BANK) for k in (0, 4)]
FIRST_OUT = len(BLOCKS)
BLOCKS += [("out", k, 4, col, BANK) for k in (4, 0) for col in (0, BANK)]
FIRST_FFN = len(BLOCKS)
FFN_CHUNKS = -(-FF // BANK)
for c in range(FF // BANK):
    BLOCKS += [(m, k, 4, c * BANK, BANK) for m in ("gate", "up") for k in (0, 4)]
BLOCKS += [(m, 0, 8, FF // BANK * BANK, 256) for m in ("gate", "up")]
FIRST_DOWN = len(BLOCKS)
KF = FF // P
KF_OWN = 20
BLOCKS += [("down", k, 2, 0, D) for k in range(0, KF, 2)]
NB = len(BLOCKS)
PROJ_COLS = [(4 * GROUP, 256), (3 * GROUP, BANK), (GROUP, BANK), (0, BANK), (2 * GROUP, BANK)]

RAW = 3
SLOTS = 4
SKIP_AT = 38
assert FIRST_DOWN < SKIP_AT <= NB - SLOTS


def slot(b, slots=SLOTS):
    return b % slots if b < SKIP_AT else (b - NB) % slots


def before(b, slots=SLOTS):
    c = b - 1
    while slot(c % NB, slots) != slot(b, slots):
        c -= 1
    return c


def freed_by(b):
    needs = [max(before(x) for x in range(c + 1)) for c in range(NB)]
    return [c for c in range(NB) if needs[c] == b]


def completes(b, t):
    m, k0, nk, col, n = BLOCKS[b]
    if m == "down":
        return [("down", t, c) for c in range(2)] if k0 + nk == KF else []
    if m == "out":
        return [("out", t, col // BANK)] if k0 == 0 else []
    if k0 + nk < D // P:
        return []
    return [("proj", (b + 1) // 2, t)] if m == "in" else [(m, col // BANK, t)]


ROUNDS = [(0, (0, 1, 2, 3)), (1, (0, 1)), (1, (2, 3))]


class Order:

    def __init__(self, names):
        self.names = list(names)
        self.at = {n: i for i, n in enumerate(self.names)}
        self.n = len(self.names)
        self.said = 0

    def tick(self, name):
        assert self.names[self.said % self.n] == name, (self.names[self.said % self.n], name)
        self.said += 1

    def before(self, L, name):
        return L * self.n + self.at[name]

    def done(self, L, name):
        return L * self.n + self.at[name] + 1


HOLDS = [[] for _ in range(8)]
for ci in range(5):
    for t in range(T):
        HOLDS[2 - 2 * t + ci % 2].append(("proj", ci, t))
for c in range(2):
    HOLDS[2 + c].append(("out", 0, c))
    HOLDS[c].append(("out", 1, c))
for c in range(FFN_CHUNKS):
    for t in range(T):
        HOLDS[2 - 2 * t].append(("gate", c, t))
        HOLDS[3 - 2 * t].append(("up", c, t))
for c in range(2):
    HOLDS[2 + c].append(("down", 0, c))
    HOLDS[c].append(("down", 1, c))
for j in range(2):
    HOLDS[4 + j].append(("ht", 0, j, 1))
    for g in (SWA, MOBA):
        for r in range(3):
            HOLDS[4 + j] += [("scores", g, r, j), ("pt", g, r, j)]
    HOLDS[4 + j].append(("ht", 1, j, 1))
HOLDS[6] += [("ht", 0, 0, 0), ("qk", 0, 0), ("qk", 1, 0), ("qk", 0, 1), ("qk", 1, 1), ("qk", 2, 0), ("qk", 2, 1),
             ("qk", 3, 0), ("qk", 3, 1), ("mix", SWA, 0), ("mix", SWA, 1), ("mix", MOBA, 0), ("mix", MOBA, 1),
             ("ht", 1, 0, 0)]
HOLDS[6] += [("ft", c, 0) for c in range(FFN_CHUNKS)]
HOLDS[7] += [("ht", 0, 1, 0), ("pv", SWA, 0), ("pv", SWA, 1), ("pv", MOBA, 0), ("pv", MOBA, 1), ("ht", 1, 1, 0)]
HOLDS[7] += [("ft", c, 1) for c in range(FFN_CHUNKS)]
BANK_OF = {name: b for b in range(8) for name in HOLDS[b]}


def trunk(nc, x_in, w_in, b_in, w_out, g_attn_pre, g_attn_post, g_moba, g_swa, sinks_in,
          g_ffn_pre, g_ffn_post, w_gate, w_up, w_down, cos_in, sin_in, out):
    depth = w_in.shape[0]
    weights = {"in": w_in, "out": w_out, "gate": w_gate, "up": w_up, "down": w_down}

    with ExitStack() as ctx:
        def sb(name, shape, dt=F32):
            return ctx.enter_context(nc.sbuf_tensor(name, shape, dt))

        def sem(name):
            return ctx.enter_context(nc.semaphore(name))

        x = sb("x", [P, T, D])
        actT = {s: sb("actT_" + s, [P, D // P, SEQ], F32R) for s in "hl"}
        fT = {s: sb("fT_" + s, [P, KF_OWN, SEQ], F32R) for s in "hl"}
        raw = sb("raw", [P, RAW, BLOCK])
        w = {s: sb("w_" + s, [P, SLOTS, BLOCK], F32R) for s in "hl"}
        bias = sb("bias", [P, 2, BANK])
        gain_ffn = bias[:].rearrange("p a n -> p (a n)")
        gain_a = sb("gain_a", [P, D])
        gain_b = sb("gain_b", [P, D])
        work = sb("work", [P, 11, BANK])
        stage = [work[:, t, :] for t in range(T)]
        roped = [work[:, 2 + t, :] for t in range(T)]
        probs = work[:, 4:6, :]
        probsT = work[:, 6:8, :]
        o = [work[:, 8 + t, :] for t in range(T)]
        rope_tmp = work[:, 10, :]
        y = [work[:, 0:2, :], work[:, 4:6, :]]
        silu = [work[:, 6 + t, :] for t in range(T)]
        f = [work[:, 8 + t, :] for t in range(T)]
        v = {MOBA: sb("v_moba", [P, T, GROUP]), SWA: sb("v_swa", [P, T, KV])}
        qT = {g: sb(f"qT_{g}", [P, 4, SEQ]) for g in (MOBA, SWA)}
        kT = {MOBA: sb("kT_0", [P, 4, SEQ]), SWA: sb("kT_1", [P, 1, SEQ])}
        ident = sb("ident", [P, P])
        ident16 = sb("ident16", [P, P], BF16)
        masks = sb("masks", [P, 4, P], BF16)
        cos = sb("cos", [P, T, HEAD // 2])
        sin = sb("sin", [P, T, HEAD // 2])
        sinks = sb("sinks", [P, 2, 4])
        neg_max = sb("neg_max", [P, 2, T, 2, 4])
        row_sum = sb("row_sum", [P, 2, T, 2, 4])
        top = sb("top", [P, 2, 4])
        sink_exp = sb("sink_exp", [P, 2, 4])
        norms = sb("norms", [P, 16])
        ss_x, rstd_x = norms[:, 0:2], norms[:, 2:4]
        ss_y, rstd_y = norms[:, 4:8].rearrange("p (t c) -> p t c", t=T), norms[:, 8:10]
        ss_o, rstd_o = norms[:, 10:12], norms[:, 12:14]
        constants = sb("constants", [P, 2])
        minus_half, eps = constants[:, 0:1], constants[:, 1:2]
        junk = [[silu[t].bitcast(BF16) for t in range(T)], [rope_tmp.bitcast(BF16)] * T]

        bank = [ctx.enter_context(nc.psum_tensor(f"bank{b}", [P, BANK], F32)) for b in range(8)]

        x_in_done = [sem(f"x_in_done{t}") for t in range(T)]
        tables_in = sem("tables_in")
        bias_in = [sem(f"bias_in{n}") for n in range(2)]
        gain_ffn_in = sem("gain_ffn_in")
        sinks_loaded = sem("sinks_loaded")
        gain_a_in = sem("gain_a_in")
        gain_b_in = sem("gain_b_in")
        raw_in = [sem(f"raw_in{r}") for r in range(RAW)]
        places_free = sem("places_free")
        out_done = sem("out_done")
        const_ready = sem("const_ready")
        hi_ready = sem("hi_ready")
        lo_ready = sem("lo_ready")
        block_used = sem("block_used")
        full = [sem(f"full{b}") for b in range(8)]
        drained = [sem(f"drained{b}") for b in range(8)]
        hiT_ready = sem("hiT_ready")
        x_ready = sem("x_ready")
        rows_ready = sem("rows_ready")
        squares_x = sem("squares_x")
        rstd_x_ready = sem("rstd_x_ready")
        squares_y = sem("squares_y")
        rstd_y_ready = sem("rstd_y_ready")
        rotated = sem("rotated")
        max_ready = sem("max_ready")
        sink_arg_ready = sem("sink_arg_ready")
        sink_exp_ready = sem("sink_exp_ready")
        probsT_used = sem("probsT_used")
        o_ready = sem("o_ready")
        rstd_o_ready = sem("rstd_o_ready")
        o_scaled = sem("o_scaled")
        eps_added = sem("eps_added")
        pool_step = sem("pool_step")
        dve_step = sem("dve_step")

        HELD = [Order(names) for names in HOLDS]
        RAW_IN = [Order([b for b in range(NB) if slot(b, RAW) == n]) for n in range(RAW)]
        USED = Order([b for b in range(NB) if not completes(b, T - 1)])
        tiles = [(ph, t) for ph in range(2) for t in range(T)]
        X_READY, ROWS, SQ_X, R_X, R_Y = (Order(tiles) for _ in range(5))
        SQ_Y = Order([(ph, t, c) for ph, t in tiles for c in range(2)])
        groups = [(SWA, 0), (SWA, 1), (MOBA, 0), (MOBA, 1)]
        O_READY, R_O, O_SCALED = (Order(groups) for _ in range(3))
        ROTATED = Order([(0, 0), (1, 0), (0, 1), (1, 1), (2, 0), (2, 1), (3, 0), (3, 1)])
        rounds = [(g, r) for g in (SWA, MOBA) for r in range(3)]
        MAX = Order(rounds)
        PV = Order([(g, r, j) for g, r in rounds for j in range(2) if r == 1 or j == 0])
        SINK_ARG, SINK_EXP = Order([0, 1]), Order([0, 1])
        HIT = Order([("ht", 0, 0, 0), ("ht", 0, 0, 1), ("ht", 0, 1, 0), ("ht", 0, 1, 1), ("mix", SWA, 0),
                     ("mix", SWA, 1), ("mix", MOBA, 0), ("mix", MOBA, 1), ("ht", 1, 0, 0), ("ht", 1, 0, 1),
                     ("ht", 1, 1, 0), ("ht", 1, 1, 1)] + [("ft", c, t) for c in range(FFN_CHUNKS) for t in range(T)])

        def transposed(name):
            if name[0] == "ht":
                return actT, 4 * name[3], 4, name[2]
            if name[0] == "mix":
                return actT, 4 * name[1], 4, name[2]
            if 4 * name[1] < KF_OWN:
                return fT, 4 * name[1], 4, name[2]
            return actT, 4 * name[1] - KF_OWN, KF - 4 * name[1], name[2]

        def tokens(t):
            return slice(t * P, (t + 1) * P)

        def broadcast(row, width):
            return row.rearrange("(a n) -> a n", a=1).broadcast_to([P, width])

        block = ctx.enter_context(nc.Block())

        @block.sync
        def _(sp):
            def place_free(sem, count):
                sp.wait_ge(sem, count)
                sp.sem_inc(places_free, 1)

            def load_block(L, b, wait=True):
                m, k, nk, col, n = BLOCKS[b]
                r = slot(b, RAW)
                if wait:
                    place_free(lo_ready, L * NB + before(b, RAW) + 1)
                sp.dma_start(raw[:, r, :].rearrange("p (k n) -> p k n", k=nk),
                             weights[m][L, k * P:(k + nk) * P, col:col + n].rearrange("(k p) n -> p k n", p=P)
                             ).then_inc(raw_in[r], 16)

            def load_bias(L, ci):
                col, n = PROJ_COLS[ci]
                sp.dma_start(bias[:, ci % 2, 0:n], broadcast(b_in[L, col:col + n], n)).then_inc(bias_in[ci % 2], 16)

            def load_sinks(L):
                sp.dma_start(sinks[:].rearrange("p j i -> p (j i)"), broadcast(sinks_in[L], HEADS)
                             ).then_inc(sinks_loaded, 16)

            def projected(L, ci, t):
                name = ("proj", ci, t)
                place_free(drained[BANK_OF[name]], HELD[BANK_OF[name]].done(L, name) + 1)

            sp.dma_start(x[:, 0, :], x_in[0, 0:P, :]).then_inc(x_in_done[0], 16)
            sp.dma_start(gain_a[:], broadcast(g_attn_pre[0], D)).then_inc(gain_a_in, 16)
            load_block(0, 0, wait=False)
            load_block(0, 1, wait=False)
            load_block(0, 2, wait=False)
            load_bias(0, 0)
            sp.dma_start(x[:, 1, :], x_in[0, P:SEQ, :]).then_inc(x_in_done[1], 16)
            load_block(0, 3)
            sp.dma_start(cos[:], cos_in.rearrange("(t p) n -> p t n", p=P)).then_inc(tables_in, 16)
            sp.dma_start(sin[:], sin_in.rearrange("(t p) n -> p t n", p=P)).then_inc(tables_in, 16)
            load_sinks(0)
            load_bias(0, 1)

            with sp.Fori(0, depth) as L:
                for b in range(RAW + 1, NB):
                    load_block(L, b)
                    if b == 6:
                        place_free(rows_ready, ROWS.done(L, (0, 1)))
                        sp.dma_start(gain_a[:, 0:GROUP], broadcast(g_moba[L], GROUP)).then_inc(gain_a_in, 16)
                        sp.dma_start(gain_a[:, GROUP:D], broadcast(g_swa[L], GROUP)).then_inc(gain_a_in, 16)
                        sp.dma_start(gain_b[:], broadcast(g_attn_post[L], D)).then_inc(gain_b_in, 16)
                    if b == 7:
                        projected(L, 0, 1)
                        load_bias(L, 2)
                    if b == 9:
                        projected(L, 1, 1)
                        load_bias(L, 3)
                    if b == 11:
                        projected(L, 2, 1)
                        load_bias(L, 4)
                    if b == 15:
                        projected(L, 4, 1)
                        sp.dma_start(gain_ffn, broadcast(g_ffn_pre[L], D)).then_inc(gain_ffn_in, 16)
                    if b == 24:
                        place_free(x_ready, X_READY.done(L, (0, 1)))
                        sp.dma_start(gain_b[:], broadcast(g_ffn_post[L], D)).then_inc(gain_b_in, 16)
                with sp.If(L < depth - 1):
                    following = nc.s_assert_within(
                        L + 1, 1, depth - 1, skip_runtime_bounds_check_because="L < depth - 1 here")
                    place_free(rows_ready, ROWS.done(L, (1, 1)))
                    sp.dma_start(gain_a[:], broadcast(g_attn_pre[following], D)).then_inc(gain_a_in, 16)
                    load_bias(following, 0)
                    load_bias(following, 1)
                    load_sinks(following)
                    for b in range(RAW + 1):
                        load_block(following, b)
            for t in range(T):
                sp.wait_ge(x_ready, X_READY.done(depth - 1, (1, t)))
                sp.dma_start(out[0, tokens(t), :], x[:, t, :]).then_inc(out_done, 16)
            sp.wait_ge(out_done, 16 * T)

        @block.gpsimd
        def _(pool):
            for b in range(8):
                pool.sem_inc(drained[b], 1)
            pool.sem_inc(block_used, USED.n)
            nc.gpsimd.memset(ident[:], 0.0).then_inc(const_ready, 1)
            nc.gpsimd.memset(ident16[:], 0.0).then_inc(const_ready, 1)
            nc.gpsimd.memset(masks[:], 0.0).then_inc(const_ready, 1)
            nc.gpsimd.memset(minus_half, -0.5).then_inc(const_ready, 1)
            nc.gpsimd.memset(eps, EPS).then_inc(const_ready, 1)
            pool.wait_ge(const_ready, 5)
            for m in (ident, ident16):
                nc.gpsimd.affine_select(out=m[:], in_=m[:], compare_op=ALU.not_equal, fill=1.0, base=0,
                                        pattern=[[-1, P]], channel_multiplier=1).then_inc(const_ready, 1)
            for n in (1, 3):
                nc.gpsimd.affine_select(out=masks[:, n, :], in_=masks[:, n, :], compare_op=ALU.is_ge, fill=NEG,
                                        base=0, pattern=[[-1, P]], channel_multiplier=1).then_inc(const_ready, 1)
            nc.gpsimd.affine_select(out=masks[:, 2, :], in_=masks[:, 2, :], compare_op=ALU.is_gt, fill=NEG,
                                    base=0, pattern=[[1, P]], channel_multiplier=-1).then_inc(const_ready, 1)

            PER_LAYER = 20
            n_step = [0]

            def link(L, ins):
                n_step[0] += 1
                ins.then_inc(pool_step, 1)
                pool.wait_ge(pool_step, L * PER_LAYER + n_step[0])

            def rotate(L, ci, t):
                if ci == 0:
                    src = stage[t][:, 0:KV].rearrange("p (j i d) -> p j i d", j=2, i=1)
                    dst = roped[t][:, 0:KV].rearrange("p (i j d) -> p j i d", j=2, i=1)
                else:
                    src = stage[t].rearrange("p (j i d) -> p j i d", j=2, i=4)
                    dst = roped[t].rearrange("p (i j d) -> p j i d", j=2, i=4)
                n = src.shape[2]
                half = HEAD // 2
                c = cos[:, t, :].unsqueeze(1).unsqueeze(1).broadcast_to([P, 2, n, half])
                s = sin[:, t, :].unsqueeze(1).unsqueeze(1).broadcast_to([P, 2, n, half])
                tmp = [rope_tmp[:, q * 256:q * 256 + 2 * n * half].rearrange("p (j i d) -> p j i d", j=2, i=n)
                       for q in range(2)]
                x1, x2 = src[:, :, :, 0:half], src[:, :, :, half:HEAD]
                pool.wait_ge(drained[BANK_OF["proj", ci, t]],
                             HELD[BANK_OF["proj", ci, t]].done(L, ("proj", ci, t)) + 1)
                if ci:
                    b = BANK_OF["qk", ci - 1, t]
                    pool.wait_ge(full[b], HELD[b].done(L, ("qk", ci - 1, t)))
                if (ci, t) != ROTATED.names[0]:
                    pool.wait_ge(rotated, ROTATED.before(L, (ci, t)))
                nc.gpsimd.tensor_tensor(dst[:, :, :, 0:half], x1, c, ALU.mult)
                nc.gpsimd.tensor_tensor(tmp[0], x2, s, ALU.mult)
                nc.gpsimd.tensor_tensor(dst[:, :, :, half:HEAD], x2, c, ALU.mult)
                link(L, nc.gpsimd.tensor_tensor(tmp[1], x1, s, ALU.mult))
                nc.gpsimd.tensor_tensor(dst[:, :, :, 0:half], dst[:, :, :, 0:half], tmp[0], ALU.subtract)
                nc.gpsimd.tensor_tensor(dst[:, :, :, half:HEAD], dst[:, :, :, half:HEAD], tmp[1], ALU.add
                                        ).then_inc(rotated, 1)
                ROTATED.tick((ci, t))

            def rms_x(L, ph, t):
                pool.wait_ge(squares_x, SQ_X.done(L, (ph, t)))
                nc.gpsimd.tensor_tensor(ss_x[:, t:t + 1], ss_x[:, t:t + 1], eps, ALU.add).then_inc(eps_added, 1)
                pool.wait_ge(eps_added, R_X.done(L, (ph, t)))
                nc.gpsimd.tensor_tensor(rstd_x[:, t:t + 1], ss_x[:, t:t + 1], minus_half, ALU.pow
                                        ).then_inc(rstd_x_ready, 1)
                R_X.tick((ph, t))

            def rms_y(L, ph, t):
                pool.wait_ge(squares_y, SQ_Y.done(L, (ph, t, 0)))
                link(L, nc.gpsimd.tensor_tensor(ss_y[:, t, 0:1], ss_y[:, t, 0:1], eps, ALU.add))
                pool.wait_ge(squares_y, SQ_Y.done(L, (ph, t, 1)))
                link(L, nc.gpsimd.tensor_tensor(ss_y[:, t, 0:1], ss_y[:, t, 0:1], ss_y[:, t, 1:2], ALU.add))
                nc.gpsimd.tensor_tensor(rstd_y[:, t:t + 1], ss_y[:, t, 0:1], minus_half, ALU.pow
                                        ).then_inc(rstd_y_ready, 1)
                R_Y.tick((ph, t))

            def rms_o(L, g, t):
                b = BANK_OF["pv", g, t]
                pool.wait_ge(drained[b], HELD[b].done(L, ("pv", g, t)) + 1)
                link(L, nc.gpsimd.tensor_tensor(ss_o[:, t:t + 1], ss_o[:, t:t + 1], eps, ALU.add))
                nc.gpsimd.tensor_tensor(rstd_o[:, t:t + 1], ss_o[:, t:t + 1], minus_half, ALU.pow
                                        ).then_inc(rstd_o_ready, 1)
                R_O.tick((g, t))

            pool.wait_ge(const_ready, 10)
            rms_x(0, 0, 0)
            pool.wait_ge(tables_in, 32)
            rms_x(0, 0, 1)
            with pool.Fori(0, depth) as L:
                rotate(L, 0, 0)
                rotate(L, 1, 0)
                rotate(L, 0, 1)
                rotate(L, 1, 1)
                rotate(L, 2, 0)
                rotate(L, 2, 1)
                rms_o(L, SWA, 0)
                rotate(L, 3, 0)
                rotate(L, 3, 1)
                rms_o(L, SWA, 1)
                rms_o(L, MOBA, 0)
                rms_o(L, MOBA, 1)
                rms_y(L, 0, 0)
                rms_x(L, 1, 0)
                rms_y(L, 0, 1)
                rms_x(L, 1, 1)
                rms_y(L, 1, 0)
                with pool.If(L < depth - 1):
                    rms_x(L + 1, 0, 0)
                rms_y(L, 1, 1)
                with pool.If(L < depth - 1):
                    rms_x(L + 1, 0, 1)
                assert n_step[0] == PER_LAYER, n_step

        @block.scalar
        def _(act):
            def hi(L, b, wait=True):
                r = slot(b, RAW)
                act.wait_ge(raw_in[r], RAW_IN[r].done(L, b) * 16)
                last = before(b)
                if last < 0 and completes(last % NB, T - 1):
                    pass
                elif completes(last % NB, T - 1):
                    name = completes(last, T - 1)[-1]
                    act.wait_ge(full[BANK_OF[name]], HELD[BANK_OF[name]].done(L, name))
                elif wait:
                    act.wait_ge(block_used, USED.done(L, last % NB) + (USED.n if last >= 0 else 0))
                nc.scalar.activation(w["h"][:, slot(b), :], raw[:, r, :], ACT.Copy).then_inc(hi_ready, 1)

            def after(L, b):
                for c in freed_by(b):
                    hi(L, c)

            def hiT(L, name):
                b = BANK_OF[name]
                dst, k, nk, t = transposed(name)
                act.wait_ge(full[b], HELD[b].done(L, name))
                nc.scalar.activation(dst["h"][:, k:k + nk, tokens(t)],
                                     bank[b][:, 0:nk * P].rearrange("p (k n) -> p k n", k=nk), ACT.Copy
                                     ).then_inc(hiT_ready, 1)
                HIT.tick(name)

            def sum_x(L, ph, t):
                nc.scalar.activation(junk[ph][t], x[:, t, :], ACT.Square, scale=D ** -0.5,
                                     accum_out=ss_x[:, t:t + 1]).then_inc(squares_x, 1)
                SQ_X.tick((ph, t))

            def sum_y(L, ph, t, halves=(0, 1)):
                for c in halves:
                    name = ("down" if ph else "out", t, c)
                    b = BANK_OF[name]
                    act.wait_ge(full[b], HELD[b].done(L, name))
                    nc.scalar.activation(y[t][:, c, :], bank[b][:], ACT.Square, scale=D ** -0.5,
                                         accum_out=ss_y[:, t, c:c + 1]).then_inc(squares_y, 1)
                    SQ_Y.tick((ph, t, c))

            def keep_qk(L, ci, t):
                b = BANK_OF["qk", ci, t]
                act.wait_ge(full[b], HELD[b].done(L, ("qk", ci, t)))
                dst = (kT[SWA], qT[SWA], kT[MOBA], qT[MOBA])[ci]
                n = dst.shape[1]
                nc.scalar.activation(dst[:, :, tokens(t)], bank[b][:, 0:n * P].rearrange("p (i n) -> p i n", i=n),
                                     ACT.Copy).then_inc(drained[b], 1)

            def exps(L, g, r):
                t, pairs = ROUNDS[r]
                keys = P * (t + 1)
                act.wait_ge(max_ready, MAX.done(L, (g, r)))
                for j in range(2):
                    if (g, r) != (SWA, 0):
                        pg, pr = rounds[rounds.index((g, r)) - 1]
                        act.wait_ge(full[4 + j], HELD[4 + j].done(L, ("pt", pg, pr, j)))
                    for n, i in enumerate(pairs):
                        last = nc.scalar.activation(probs[:, j, n * keys:(n + 1) * keys],
                                                    bank[4 + j][:, n * keys:(n + 1) * keys], ACT.Exp,
                                                    bias=neg_max[:, g, t, j, i:i + 1], scale=SCALE,
                                                    accum_out=row_sum[:, g, t, j, i:i + 1])
                    last.then_inc(drained[4 + j], 1)

            def keep_probsT(L, g, r):
                act.wait_ge(full[4], HELD[4].done(L, ("pt", g, r, 0)))
                if (g, r) != (SWA, 0):
                    pg, pr = rounds[rounds.index((g, r)) - 1]
                    act.wait_ge(probsT_used, PV.done(L, (pg, pr, 0)))
                nc.scalar.activation(probsT[:, 0, :], bank[4][:], ACT.Copy).then_inc(drained[4], 1)

            def sink_exps(L, t):
                act.wait_ge(sink_arg_ready, SINK_ARG.done(L, t))
                nc.scalar.activation(sink_exp[:], sink_exp[:], ACT.Exp).then_inc(sink_exp_ready, 1)
                SINK_EXP.tick(t)

            def sum_o(L, g, t):
                b = BANK_OF["pv", g, t]
                act.wait_ge(o_ready, O_READY.done(L, (g, t)))
                nc.scalar.activation(bank[b][:], o[t], ACT.Square, scale=GROUP ** -0.5, accum_out=ss_o[:, t:t + 1]
                                     ).then_inc(drained[b], 1)

            def silus(L, c, t):
                n = min(BANK, FF - c * BANK)
                b = BANK_OF["gate", c, t]
                act.wait_ge(full[b], HELD[b].done(L, ("gate", c, t)))
                if c == 0:
                    act.wait_ge(rstd_x_ready, R_X.done(L, (1, t)))
                else:
                    bu = BANK_OF["up", c - 1, t]
                    act.wait_ge(drained[bu], HELD[bu].done(L, ("up", c - 1, t)) + 1)
                nc.scalar.activation(silu[t][:, 0:n], bank[b][:, 0:n], ACT.Silu, scale=rstd_x[:, t:t + 1]
                                     ).then_inc(drained[b], 1)

            act.wait_ge(x_in_done[0], 16)
            sum_x(0, 0, 0)
            hiT(0, ("ht", 0, 0, 0))
            hi(0, 0, wait=False)
            hiT(0, ("ht", 0, 0, 1))
            hi(0, 1, wait=False)
            hi(0, 2, wait=False)
            act.wait_ge(x_in_done[1], 16)
            sum_x(0, 0, 1)
            hi(0, 3)
            with act.Fori(0, depth) as L:
                hiT(L, ("ht", 0, 1, 0))
                hiT(L, ("ht", 0, 1, 1))
                keep_qk(L, 0, 0)
                keep_qk(L, 1, 0)
                after(L, 0)
                after(L, 1)
                after(L, 2)
                exps(L, SWA, 0)
                sink_exps(L, 0)
                keep_qk(L, 0, 1)
                keep_probsT(L, SWA, 0)
                after(L, 3)
                keep_qk(L, 1, 1)
                after(L, 4)
                exps(L, SWA, 1)
                sum_o(L, SWA, 0)
                keep_probsT(L, SWA, 1)
                keep_qk(L, 2, 0)
                exps(L, SWA, 2)
                sink_exps(L, 1)
                after(L, 5)
                keep_qk(L, 2, 1)
                keep_probsT(L, SWA, 2)
                after(L, 6)
                keep_qk(L, 3, 0)
                sum_o(L, SWA, 1)
                keep_qk(L, 3, 1)
                exps(L, MOBA, 0)
                hiT(L, ("mix", SWA, 0))
                keep_probsT(L, MOBA, 0)
                after(L, 7)
                exps(L, MOBA, 1)
                hiT(L, ("mix", SWA, 1))
                sum_o(L, MOBA, 0)
                keep_probsT(L, MOBA, 1)
                after(L, 8)
                hiT(L, ("mix", MOBA, 0))
                exps(L, MOBA, 2)
                keep_probsT(L, MOBA, 2)
                sum_o(L, MOBA, 1)
                sum_y(L, 0, 0)
                after(L, 9)
                hiT(L, ("mix", MOBA, 1))
                act.wait_ge(x_ready, X_READY.done(L, (0, 0)))
                sum_x(L, 1, 0)
                after(L, 10)
                hiT(L, ("ht", 1, 0, 0))
                hiT(L, ("ht", 1, 0, 1))
                sum_y(L, 0, 1, (0,))
                after(L, 11)
                sum_y(L, 0, 1, (1,))
                after(L, 12)
                act.wait_ge(x_ready, X_READY.done(L, (0, 1)))
                sum_x(L, 1, 1)
                hiT(L, ("ht", 1, 1, 0))
                hiT(L, ("ht", 1, 1, 1))
                silus(L, 0, 0)
                after(L, 13)
                after(L, 14)
                silus(L, 0, 1)
                after(L, 15)
                after(L, 16)
                for c in range(1, FFN_CHUNKS):
                    b = FIRST_FFN + 4 * c
                    hiT(L, ("ft", c - 1, 0))
                    after(L, b)
                    hiT(L, ("ft", c - 1, 1))
                    silus(L, c, 0)
                    silus(L, c, 1)
                    for q in range(1, 2 if c == FFN_CHUNKS - 1 else 4):
                        after(L, b + q)
                hiT(L, ("ft", FFN_CHUNKS - 1, 0))
                after(L, FIRST_DOWN)
                hiT(L, ("ft", FFN_CHUNKS - 1, 1))
                for b in range(FIRST_DOWN + 1, NB - 4):
                    after(L, b)
                sum_y(L, 1, 0)
                with act.If(L < depth - 1):
                    hi(L + 1, 0)
                    act.wait_ge(x_ready, X_READY.done(L, (1, 0)))
                    sum_x(L + 1, 0, 0)
                    hiT(L + 1, ("ht", 0, 0, 0))
                    hiT(L + 1, ("ht", 0, 0, 1))
                    hi(L + 1, 1)
                    hi(L + 1, 2)
                sum_y(L, 1, 1)
                with act.If(L < depth - 1):
                    hi(L + 1, 3)
                    act.wait_ge(x_ready, X_READY.done(L, (1, 1)))
                    sum_x(L + 1, 0, 1)

        @block.vector
        def _(dve):
            PER_LAYER = 15
            n_step = [0]

            def link(L, ins):
                n_step[0] += 1
                ins.then_inc(dve_step, 1)
                dve.wait_ge(dve_step, L * PER_LAYER + n_step[0])

            def lo(L, b):
                dve.wait_ge(hi_ready, L * NB + b + 1)
                nc.vector.tensor_tensor(w["l"][:, slot(b), :], raw[:, slot(b, RAW), :],
                                        w["h"][:, slot(b), :].bitcast(F32), ALU.subtract).then_inc(lo_ready, 1)

            def after(L, b):
                for c in freed_by(b):
                    lo(L, c)

            def loT(L, name):
                b = BANK_OF[name]
                dst, k, nk, t = transposed(name)
                dve.wait_ge(hiT_ready, HIT.done(L, name))
                nc.vector.tensor_tensor(dst["l"][:, k:k + nk, tokens(t)],
                                        bank[b][:, 0:nk * P].rearrange("p (k n) -> p k n", k=nk),
                                        dst["h"][:, k:k + nk, tokens(t)].bitcast(F32), ALU.subtract
                                        ).then_inc(drained[b], 1)

            def scale_rows(L, ph, t):
                if ph == 0:
                    dve.wait_ge(gain_a_in, (L * 3 + 1) * 16)
                else:
                    dve.wait_ge(gain_ffn_in, (L + 1) * 16)
                gain = gain_ffn if ph else gain_a[:]
                nc.vector.tensor_tensor(y[t].rearrange("p a n -> p (a n)"), x[:, t, :], gain, ALU.mult
                                        ).then_inc(rows_ready, 1)
                ROWS.tick((ph, t))

            def project(L, ci, t):
                b = BANK_OF["proj", ci, t]
                n = PROJ_COLS[ci][1]
                if t == 0:
                    dve.wait_ge(bias_in[ci % 2], (L * (3 - ci % 2) + ci // 2 + 1) * 16)
                if ci == 0:
                    dve.wait_ge(rstd_x_ready, R_X.done(L, (0, t)))
                dve.wait_ge(full[b], HELD[b].done(L, ("proj", ci, t)))
                if 0 < ci < 4:
                    dve.wait_ge(rotated, ROTATED.done(L, (ci - 1, t)))
                dst = v[MOBA][:, t, :] if ci == 4 else stage[t][:, 0:n]
                if ci == 0:
                    n = KV
                    nc.vector.scalar_tensor_tensor(v[SWA][:, t, :], bank[b][:, KV:2 * KV], rstd_x[:, t:t + 1],
                                                   bias[:, 0, KV:2 * KV], ALU.mult, ALU.add)
                nc.vector.scalar_tensor_tensor(dst[:, 0:n], bank[b][:, 0:n], rstd_x[:, t:t + 1],
                                               bias[:, ci % 2, 0:n], ALU.mult, ALU.add).then_inc(drained[b], 1)

            def maxima(L, g, r):
                t, pairs = ROUNDS[r]
                n = len(pairs)
                i = slice(pairs[0], pairs[0] + n)
                for j in range(2):
                    dve.wait_ge(full[4 + j], HELD[4 + j].done(L, ("scores", g, r, j)))
                    ins = nc.vector.tensor_reduce(top[:, j, i], bank[4 + j][:].rearrange("p (i n) -> p i n", i=n),
                                                  AX.X, ALU.max)
                link(L, ins)
                if g == SWA:
                    if r == 0:
                        dve.wait_ge(sinks_loaded, (L + 1) * 16)
                    link(L, nc.vector.scalar_tensor_tensor(top[:, :, i], top[:, :, i], SCALE, sinks[:, :, i],
                                                           ALU.mult, ALU.max))
                    ins = nc.vector.tensor_scalar(neg_max[:, g, t, :, i], top[:, :, i], -1.0, None, ALU.mult)
                else:
                    ins = nc.vector.tensor_scalar(neg_max[:, g, t, :, i], top[:, :, i], -SCALE, None, ALU.mult)
                ins.then_inc(max_ready, 1)
                MAX.tick((g, r))
                if g == SWA and r != 1:
                    dve.wait_ge(max_ready, MAX.done(L, (g, r)))
                    nc.vector.tensor_tensor(sink_exp[:], sinks[:], neg_max[:, g, t, :, :], ALU.add
                                            ).then_inc(sink_arg_ready, 1)
                    SINK_ARG.tick(t)

            def keep_probsT(L, g, r):
                dve.wait_ge(full[5], HELD[5].done(L, ("pt", g, r, 1)))
                if (g, r) != (SWA, 0):
                    pg, pr = rounds[rounds.index((g, r)) - 1]
                    if pr != 1:
                        dve.wait_ge(full[7], HELD[7].done(L, ("pv", pg, ROUNDS[pr][0])))
                    else:
                        dve.wait_ge(probsT_used, PV.done(L, (pg, pr, 1)))
                nc.vector.tensor_copy(probsT[:, 1, :], bank[5][:]).then_inc(drained[5], 1)

            def normalise(L, g, t):
                b = BANK_OF["pv", g, t]
                sums = row_sum[:, g, t, :, :].rearrange("p j i -> p (j i)")
                dve.wait_ge(full[b], HELD[b].done(L, ("pv", g, t)))
                if g == SWA:
                    dve.wait_ge(sink_exp_ready, SINK_EXP.done(L, t))
                    link(L, nc.vector.tensor_tensor(sums, sums, sink_exp[:].rearrange("p j i -> p (j i)"), ALU.add))
                link(L, nc.vector.reciprocal(sums, sums))
                nc.vector.tensor_tensor(o[t].rearrange("p (h d) -> p h d", h=HEADS),
                                        bank[b][:].rearrange("p (h d) -> p h d", h=HEADS),
                                        sums.unsqueeze(2).broadcast_to([P, HEADS, HEAD]), ALU.mult
                                        ).then_inc(o_ready, 1)
                O_READY.tick((g, t))

            def scale_o(L, g, t):
                if (g, t) == (SWA, 0):
                    dve.wait_ge(gain_a_in, (L * 3 + 3) * 16)
                dve.wait_ge(rstd_o_ready, R_O.done(L, (g, t)))
                nc.vector.scalar_tensor_tensor(o[t], o[t], rstd_o[:, t:t + 1], gain_a[:, g * GROUP:(g + 1) * GROUP],
                                               ALU.mult, ALU.mult).then_inc(o_scaled, 1)
                O_SCALED.tick((g, t))

            def scale_y(L, ph, t):
                for c in range(2):
                    name = ("down" if ph else "out", t, c)
                    b = BANK_OF[name]
                    if (t, c) == (0, 0):
                        dve.wait_ge(gain_b_in, (L * 2 + ph + 1) * 16)
                    dve.wait_ge(squares_y, SQ_Y.done(L, (ph, t, c)))
                    nc.vector.tensor_tensor(y[t][:, c, :], bank[b][:], gain_b[:, c * BANK:(c + 1) * BANK], ALU.mult
                                            ).then_inc(drained[b], 1)

            def update_x(L, ph, t):
                b = BANK_OF["down" if ph else "out", t, 1]
                dve.wait_ge(drained[b], HELD[b].done(L, ("down" if ph else "out", t, 1)) + 1)
                dve.wait_ge(rstd_y_ready, R_Y.done(L, (ph, t)))
                nc.vector.scalar_tensor_tensor(x[:, t, :], y[t].rearrange("p a n -> p (a n)"), rstd_y[:, t:t + 1],
                                               x[:, t, :], ALU.mult, ALU.add).then_inc(x_ready, 1)
                X_READY.tick((ph, t))

            def swiglu(L, c, t):
                n = min(BANK, FF - c * BANK)
                b = BANK_OF["up", c, t]
                dve.wait_ge(full[b], HELD[b].done(L, ("up", c, t)))
                bg = BANK_OF["gate", c, t]
                dve.wait_ge(drained[bg], HELD[bg].done(L, ("gate", c, t)) + 1)
                if c:
                    bt = BANK_OF["ft", c - 1, t]
                    dve.wait_ge(full[bt], HELD[bt].done(L, ("ft", c - 1, t)))
                nc.vector.scalar_tensor_tensor(f[t][:, 0:n], bank[b][:, 0:n], rstd_x[:, t:t + 1], silu[t][:, 0:n],
                                               ALU.mult, ALU.mult).then_inc(drained[b], 1)

            dve.wait_ge(x_in_done[0], 16)
            scale_rows(0, 0, 0)
            loT(0, ("ht", 0, 0, 0))
            lo(0, 0)
            loT(0, ("ht", 0, 0, 1))
            lo(0, 1)
            lo(0, 2)
            dve.wait_ge(x_in_done[1], 16)
            scale_rows(0, 0, 1)
            with dve.Fori(0, depth) as L:
                project(L, 0, 0)
                lo(L, 3)
                project(L, 1, 0)
                loT(L, ("ht", 0, 1, 0))
                loT(L, ("ht", 0, 1, 1))
                project(L, 0, 1)
                after(L, 0)
                after(L, 1)
                maxima(L, SWA, 0)
                project(L, 1, 1)
                after(L, 2)
                keep_probsT(L, SWA, 0)
                after(L, 3)
                project(L, 2, 0)
                normalise(L, SWA, 0)
                project(L, 2, 1)
                maxima(L, SWA, 1)
                after(L, 4)
                keep_probsT(L, SWA, 1)
                project(L, 3, 0)
                maxima(L, SWA, 2)
                scale_o(L, SWA, 0)
                keep_probsT(L, SWA, 2)
                after(L, 5)
                project(L, 3, 1)
                after(L, 6)
                normalise(L, SWA, 1)
                maxima(L, MOBA, 0)
                project(L, 4, 0)
                scale_o(L, SWA, 1)
                loT(L, ("mix", SWA, 0))
                keep_probsT(L, MOBA, 0)
                after(L, 7)
                normalise(L, MOBA, 0)
                maxima(L, MOBA, 1)
                project(L, 4, 1)
                loT(L, ("mix", SWA, 1))
                keep_probsT(L, MOBA, 1)
                scale_o(L, MOBA, 0)
                after(L, 8)
                loT(L, ("mix", MOBA, 0))
                maxima(L, MOBA, 2)
                keep_probsT(L, MOBA, 2)
                normalise(L, MOBA, 1)
                scale_y(L, 0, 0)
                scale_o(L, MOBA, 1)
                update_x(L, 0, 0)
                loT(L, ("mix", MOBA, 1))
                dve.wait_ge(x_ready, X_READY.done(L, (0, 0)))
                scale_rows(L, 1, 0)
                after(L, 9)
                loT(L, ("ht", 1, 0, 0))
                loT(L, ("ht", 1, 0, 1))
                after(L, 10)
                after(L, 11)
                scale_y(L, 0, 1)
                update_x(L, 0, 1)
                dve.wait_ge(x_ready, X_READY.done(L, (0, 1)))
                scale_rows(L, 1, 1)
                after(L, 12)
                loT(L, ("ht", 1, 1, 0))
                loT(L, ("ht", 1, 1, 1))
                after(L, 13)
                after(L, 14)
                swiglu(L, 0, 0)
                after(L, 15)
                swiglu(L, 0, 1)
                after(L, 16)
                for c in range(1, FFN_CHUNKS):
                    b = FIRST_FFN + 4 * c
                    end = b + (1 if c == FFN_CHUNKS - 1 else 3)
                    loT(L, ("ft", c - 1, 0))
                    after(L, b)
                    loT(L, ("ft", c - 1, 1))
                    for q in range(b + 1, end):
                        after(L, q)
                    swiglu(L, c, 0)
                    swiglu(L, c, 1)
                    after(L, end)
                loT(L, ("ft", FFN_CHUNKS - 1, 0))
                after(L, FIRST_DOWN)
                loT(L, ("ft", FFN_CHUNKS - 1, 1))
                for b in range(FIRST_DOWN + 1, NB - 4):
                    after(L, b)
                scale_y(L, 1, 0)
                update_x(L, 1, 0)
                with dve.If(L < depth - 1):
                    dve.wait_ge(x_ready, X_READY.done(L, (1, 0)))
                    scale_rows(L + 1, 0, 0)
                    lo(L + 1, 0)
                    loT(L + 1, ("ht", 0, 0, 0))
                    loT(L + 1, ("ht", 0, 0, 1))
                    lo(L + 1, 1)
                    lo(L + 1, 2)
                scale_y(L, 1, 1)
                update_x(L, 1, 1)
                with dve.If(L < depth - 1):
                    dve.wait_ge(x_ready, X_READY.done(L, (1, 1)))
                    scale_rows(L + 1, 0, 1)
                assert n_step[0] == PER_LAYER, n_step

        @block.tensor
        def _(pe):
            def claim(L, name):
                b = BANK_OF[name]
                HELD[b].tick(name)
                pe.wait_ge(drained[b], HELD[b].before(L, name) + 1)
                return bank[b]

            def landed(L, name):
                b = BANK_OF[name]
                pe.wait_ge(drained[b], HELD[b].done(L, name) + 1)

            def multiply(L, t, b, halves=(0, 1)):
                m, k0, nk, col, n = BLOCKS[b]
                first = k0 == (4 if m == "out" else 0)
                final = completes(b, t)
                if m == "in":
                    names = [("proj", (b + 1) // 2, t)]
                elif m == "down":
                    names = [("down", t, c) for c in range(2)]
                elif m == "out":
                    names = [("out", t, col // BANK)]
                else:
                    names = [(m, col // BANK, t)]
                if halves[0] == 0:
                    if t == 0:
                        pe.wait_ge(lo_ready, L * NB + b + 1)
                    if first:
                        for name in names:
                            claim(L, name)
                left, at = (fT, k0) if m == "down" else (actT, k0)
                if m == "down" and k0 >= KF_OWN:
                    left, at = actT, k0 - KF_OWN
                n = min(n, BANK)
                right = {s: w[s][:, slot(b), :].rearrange("p (k n) -> p k n", k=nk) for s in "hl"}
                steps = [(k, s, r, name) for k in range(halves[0] * nk // 2, (halves[-1] + 1) * nk // 2)
                         for s, r in (("h", "h"), ("h", "l"), ("l", "h")) for name in names]
                if final:
                    steps.sort(key=lambda step: names.index(step[3]))
                for k, s, r, name in steps:
                    c = name[2] if m == "down" else 0
                    ins = nc.tensor.matmul(bank[BANK_OF[name]][:, 0:n], left[s][:, at + k, tokens(t)],
                                           right[r][:, k, c * BANK:c * BANK + n],
                                           start=first and k == 0 and (s, r) == ("h", "h"),
                                           stop=name in final and k == nk - 1 and (s, r) == ("l", "h"))
                    if name in final and k == nk - 1 and (s, r) == ("l", "h"):
                        ins.then_inc(full[BANK_OF[name]], 1)
                if t == T - 1 and halves[-1] == 1 and not final:
                    ins.then_inc(block_used, 1)
                    USED.tick(b)

            def transpose(L, name, src, n):
                out_ = claim(L, name)
                for q in range(n):
                    ins = nc.tensor.transpose(out_[:, q * P:(q + 1) * P], src(q), ident[:])
                ins.then_inc(full[BANK_OF[name]], 1)

            def rows(L, ph, t):
                pe.wait_ge(rows_ready, ROWS.done(L, (ph, t)))
                for half in range(2):
                    transpose(L, ("ht", ph, t, half), lambda q: y[t][:, half, q * P:(q + 1) * P], 4)

            def qk(L, ci, t):
                pe.wait_ge(rotated, ROTATED.done(L, (ci, t)))
                transpose(L, ("qk", ci, t), lambda q: roped[t][:, q * P:(q + 1) * P], 1 if ci == 0 else 4)

            def scores(L, g, r):
                t, pairs = ROUNDS[r]
                keys = P * (t + 1)
                last_q, last_k = (("qk", 1, t), ("qk", 0, t)) if g == SWA else (("qk", 3, t), ("qk", 2, t))
                for name in (last_q, last_k):
                    landed(L, name)
                for j in range(2):
                    out_ = claim(L, ("scores", g, r, j))
                    if t == 0:
                        mask = masks[:, 1:2, :]
                    elif g == MOBA:
                        mask = masks[:, 0:2, :]
                    else:
                        mask = masks[:, 2:4, :]
                    mask = mask.rearrange("p a n -> p (a n)").unsqueeze(1).broadcast_to([P, len(pairs), keys])
                    nc.tensor.matmul(out_[:].rearrange("p (i n) -> p i n", i=len(pairs)), ident16[:], mask,
                                     start=True, stop=False)
                for n, i in enumerate(pairs):
                    for j in range(2):
                        side = slice(j * HEAD, (j + 1) * HEAD)
                        last = n == len(pairs) - 1
                        ins = nc.tensor.matmul(bank[4 + j][:, n * keys:(n + 1) * keys], qT[g][side, i, tokens(t)],
                                               kT[g][side, i if g == MOBA else 0, 0:keys], start=False, stop=last)
                        if last:
                            ins.then_inc(full[4 + j], 1)

            def probs_transposed(L, g, r, j):
                pe.wait_ge(drained[4 + j], HELD[4 + j].done(L, ("scores", g, r, j)) + 1)
                transpose(L, ("pt", g, r, j), lambda q: probs[:, j, q * P:(q + 1) * P], 4)

            def values(L, g, r, j):
                t, pairs = ROUNDS[r]
                if r < 2 and j == 0:
                    claim(L, ("pv", g, t))
                landed(L, ("pt", g, r, j))
                b = BANK_OF["pv", g, t]
                blocks = t + 1
                if j == 0:
                    ci = 0 if g == SWA else 4
                    landed(L, ("proj", ci, t))
                for n, i in enumerate(pairs):
                    h = 4 * j + i
                    cols = slice(h * HEAD, (h + 1) * HEAD) if g == MOBA else slice(j * HEAD, (j + 1) * HEAD)
                    for kb in range(blocks):
                        at = (n * blocks + kb) * P
                        ins = nc.tensor.matmul(bank[b][:, h * HEAD:(h + 1) * HEAD], probsT[:, j, at:at + P],
                                               v[g][:, kb, cols], start=kb == 0, stop=kb == blocks - 1)
                if j == 1 and r != 1:
                    ins.then_inc(full[b], 1)
                else:
                    ins.then_inc(probsT_used, 1)
                    PV.tick((g, r, j))

            def mix(L, g, t):
                pe.wait_ge(o_scaled, O_SCALED.done(L, (g, t)))
                transpose(L, ("mix", g, t), lambda q: o[t][:, q * P:(q + 1) * P], 4)

            def f_transposed(L, c, t):
                b = BANK_OF["up", c, t]
                pe.wait_ge(drained[b], HELD[b].done(L, ("up", c, t)) + 1)
                transpose(L, ("ft", c, t), lambda q: f[t][:, q * P:(q + 1) * P], min(4, KF - 4 * c))

            def rows_landed(L, ph, t):
                for half in range(2):
                    landed(L, ("ht", ph, t, half))

            pe.wait_ge(const_ready, 10)
            rows(0, 0, 0)
            with pe.Fori(0, depth) as L:
                rows_landed(L, 0, 0)
                multiply(L, 0, 0)
                multiply(L, 0, 1)
                multiply(L, 0, 2)
                rows(L, 0, 1)
                qk(L, 0, 0)
                multiply(L, 0, 3)
                rows_landed(L, 0, 1)
                multiply(L, 1, 0)
                qk(L, 1, 0)
                multiply(L, 1, 1)
                multiply(L, 1, 2)
                scores(L, SWA, 0)
                multiply(L, 1, 3)
                qk(L, 0, 1)
                multiply(L, 0, 4, (0,))
                probs_transposed(L, SWA, 0, 0)
                multiply(L, 0, 4, (1,))
                probs_transposed(L, SWA, 0, 1)
                multiply(L, 1, 4, (0,))
                values(L, SWA, 0, 0)
                values(L, SWA, 0, 1)
                qk(L, 1, 1)
                multiply(L, 1, 4, (1,))
                scores(L, SWA, 1)
                multiply(L, 0, 5)
                multiply(L, 0, 6, (0,))
                probs_transposed(L, SWA, 1, 0)
                probs_transposed(L, SWA, 1, 1)
                qk(L, 2, 0)
                multiply(L, 0, 6, (1,))
                values(L, SWA, 1, 0)
                values(L, SWA, 1, 1)
                scores(L, SWA, 2)
                multiply(L, 1, 5)
                qk(L, 2, 1)
                multiply(L, 1, 6, (0,))
                probs_transposed(L, SWA, 2, 0)
                probs_transposed(L, SWA, 2, 1)
                multiply(L, 1, 6, (1,))
                values(L, SWA, 2, 0)
                values(L, SWA, 2, 1)
                multiply(L, 0, 7)
                qk(L, 3, 0)
                multiply(L, 0, 8, (0,))
                scores(L, MOBA, 0)
                qk(L, 3, 1)
                multiply(L, 0, 8, (1,))
                multiply(L, 1, 7, (0,))
                mix(L, SWA, 0)
                multiply(L, 1, 7, (1,))
                probs_transposed(L, MOBA, 0, 0)
                probs_transposed(L, MOBA, 0, 1)
                multiply(L, 1, 8, (0,))
                values(L, MOBA, 0, 0)
                multiply(L, 1, 8, (1,))
                values(L, MOBA, 0, 1)
                scores(L, MOBA, 1)
                landed(L, ("mix", SWA, 0))
                multiply(L, 0, 9, (0,))
                mix(L, SWA, 1)
                multiply(L, 0, 9, (1,))
                probs_transposed(L, MOBA, 1, 0)
                probs_transposed(L, MOBA, 1, 1)
                multiply(L, 0, 10, (0,))
                values(L, MOBA, 1, 0)
                values(L, MOBA, 1, 1)
                mix(L, MOBA, 0)
                scores(L, MOBA, 2)
                multiply(L, 0, 10, (1,))
                landed(L, ("mix", MOBA, 0))
                multiply(L, 0, 11)
                probs_transposed(L, MOBA, 2, 0)
                probs_transposed(L, MOBA, 2, 1)
                multiply(L, 0, 12, (0,))
                values(L, MOBA, 2, 0)
                values(L, MOBA, 2, 1)
                multiply(L, 0, 12, (1,))
                landed(L, ("mix", SWA, 1))
                multiply(L, 1, 9)
                multiply(L, 1, 10, (0,))
                mix(L, MOBA, 1)
                multiply(L, 1, 10, (1,))
                landed(L, ("mix", MOBA, 1))
                multiply(L, 1, 11, (0,))
                rows(L, 1, 0)
                multiply(L, 1, 11, (1,))
                multiply(L, 1, 12)
                rows_landed(L, 1, 0)
                b = FIRST_FFN
                multiply(L, 0, b)
                multiply(L, 0, b + 1)
                multiply(L, 0, b + 2)
                rows(L, 1, 1)
                multiply(L, 0, b + 3)
                rows_landed(L, 1, 1)
                multiply(L, 1, b)
                multiply(L, 1, b + 1)
                multiply(L, 1, b + 2)
                multiply(L, 1, b + 3)
                for c in range(1, FFN_CHUNKS):
                    b = FIRST_FFN + 4 * c
                    multiply(L, 0, b)
                    f_transposed(L, c - 1, 0)
                    multiply(L, 1, b)
                    f_transposed(L, c - 1, 1)
                    for q in range(1, 2 if c == FFN_CHUNKS - 1 else 4):
                        multiply(L, 0, b + q)
                        multiply(L, 1, b + q)
                for t in range(T):
                    landed(L, ("ft", FFN_CHUNKS - 2, t))
                for b in range(FIRST_DOWN, NB - 4):
                    multiply(L, 0, b)
                    if b == FIRST_DOWN:
                        f_transposed(L, FFN_CHUNKS - 1, 0)
                    multiply(L, 1, b)
                    if b == FIRST_DOWN:
                        f_transposed(L, FFN_CHUNKS - 1, 1)
                for t in range(T):
                    landed(L, ("ft", FFN_CHUNKS - 1, t))
                for b in range(NB - 4, NB):
                    multiply(L, 0, b)
                for b in range(NB - 4, NB):
                    if b == NB - 2:
                        with pe.If(L < depth - 1):
                            rows(L + 1, 0, 0)
                    multiply(L, 1, b)


def kernel(**inputs):
    import numpy as np
    import concourse.bacc as bacc
    from concourse.bass_utils import run_bass_kernel_spmd as run

    nc = bacc.Bacc("TRN2", target_bir_lowering=False, num_devices=1)
    names = ["x", "w_in", "b_in", "w_out", "g_attn_pre", "g_attn_post", "g_moba_out", "g_swa_out",
             "attn_sinks", "g_ffn_pre", "g_ffn_post", "w_gate", "w_up", "w_down"]
    arrays = {n: np.ascontiguousarray(inputs[n]) for n in names}
    steps = np.arange(0, HEAD, 2, dtype=np.float32) / np.float32(HEAD)
    inverse = np.float32(1.0) / np.float32(10000.0) ** steps
    angle = np.arange(SEQ, dtype=np.float32)[:, None] * inverse[None, :]
    arrays["rope_cos"] = np.cos(angle)
    arrays["rope_sin"] = np.sin(angle)
    args = [nc.dram_tensor("in_" + n, a.shape, mybir.dt.from_np(a.dtype), kind="ExternalInput").ap()
            for n, a in arrays.items()]
    args.append(nc.dram_tensor("out", (1, SEQ, D), F32, kind="ExternalOutput").ap())
    trunk(nc, *args)
    got = run(nc, [{"in_" + n: a for n, a in arrays.items()}], core_ids=[0])
    return got.results[0]["out"]
```
